# Optimizing a Trainium2 kernel written in Bass

```python
import jax, jax.numpy as jnp
from jax import lax
import numpy as np

D_MODEL = 1024
BATCH = 1
SEQ = 128
DEPTH = 4
DEC_BATCH = 1
DEC_SEQ = 1024
PAST_LEN = 128

GRID_W = 64
N_MIXERS = 3
D_INNER = D_MODEL
RMS_EPS = 1e-6
RWKV_HEAD = 64
RWKV_HEADS = D_INNER // RWKV_HEAD
DECAY_LORA = 64
ICL_LORA = 64
GN_EPS = 64e-5
HEAD_DIM = 64
N_HEADS = D_INNER // HEAD_DIM
KV_HEADS = 4
Q_PER_KV = N_HEADS // KV_HEADS
ROPE_FREQS = HEAD_DIM // 4
ROPE_BASE = 10000.0
Q_BLOCK = 128
ATTN_IN_COLS = (N_HEADS + 2 * KV_HEADS) * HEAD_DIM + D_INNER
CONV_W = 3
N_LAYERS_A = (DEPTH + 2) // 3
N_LAYERS_B = (DEPTH + 1) // 3
N_LAYERS_C = DEPTH // 3

kernel_name = 'hybrid_rwkv7_gqa_shortconv_diffusion_step'

def rmsnorm(x, w):
    x32 = x.astype(jnp.float32)
    y = x32 * lax.rsqrt(jnp.mean(x32 * x32, axis=-1, keepdims=True) + RMS_EPS)
    return (y * w.astype(jnp.float32)).astype(x.dtype)

def neighbours(x):
    z = jnp.zeros_like(x[:, :1])
    prev = jnp.concatenate([z, x[:, :-1]], axis=1)
    nxt = jnp.concatenate([x[:, 1:], z], axis=1)
    return prev, nxt

def axial_rope_tables(rows):
    row = jnp.repeat(jnp.arange(rows), GRID_W)
    col = jnp.tile(jnp.arange(GRID_W), rows)
    inv = ROPE_BASE ** (-jnp.arange(ROPE_FREQS, dtype=jnp.float32) / ROPE_FREQS)
    ang = jnp.stack([row, col], axis=-1).astype(jnp.float32)[:, :, None] * inv
    return jnp.cos(ang), jnp.sin(ang)

def rope2d(x, cos, sin):
    xa = x.astype(jnp.float32).reshape(x.shape[:-1] + (2, 2, ROPE_FREQS))
    x1, x2 = xa[..., 0, :], xa[..., 1, :]
    c, s = cos[:, None], sin[:, None]
    out = jnp.stack([x1 * c - x2 * s, x2 * c + x1 * s], axis=-2)
    return out.reshape(x.shape).astype(x.dtype)

def block_attention(q, k, v):
    b, s = q.shape[:2]
    nb = s // Q_BLOCK
    qb = q.reshape(b, nb, Q_BLOCK, KV_HEADS, Q_PER_KV, HEAD_DIM).swapaxes(0, 1)
    scale = HEAD_DIM ** -0.5

    def one_block(qi):
        sc = jnp.einsum('bqkgd,btkd->bkgqt', qi, k).astype(jnp.float32) * scale
        pr = jax.nn.softmax(sc, axis=-1).astype(v.dtype)
        return jnp.einsum('bkgqt,btkd->bqkgd', pr, v)

    o = lax.map(one_block, qb)
    return o.swapaxes(0, 1).reshape(b, s, N_HEADS * HEAD_DIM)

def bidir_delta_scan(r, w, k, v, kk, a, s0):
    def orient(t):
        return jnp.concatenate([t[:, :, :1], jnp.flip(t[:, :, 1:], axis=1)], axis=2)

    xs = tuple(jnp.moveaxis(orient(t), 1, 0) for t in (r, w, k, v, kk, a))

    def step(S, inp):
        r_t, w_t, k_t, v_t, kk_t, a_t = inp
        sa = jnp.einsum('bdhvk,bdhk->bdhv', S, -kk_t)
        S = (S * w_t[..., None, :] + sa[..., None] * (kk_t * a_t)[..., None, :]
             + v_t[..., None] * k_t[..., None, :])
        return S, jnp.einsum('bdhvk,bdhk->bdhv', S, r_t)

    s_final, ys = lax.scan(step, s0, xs)
    return orient(jnp.moveaxis(ys, 0, 1)), s_final

def rwkv_mixer(h, p, j, s0):
    b, s, _ = h.shape
    prev, nxt = neighbours(h)
    xx = 0.5 * (prev + nxt) - h
    xs = h[:, :, None, :] + xx[:, :, None, :] * p['rwkv_mu'][j]
    rkvg = jnp.einsum('bsmd,mde->bsme', xs[:, :, :4], p['rwkv_w_in'][j])
    r, k, v, g = rkvg[:, :, 0], rkvg[:, :, 1], rkvg[:, :, 2], rkvg[:, :, 3]
    xw, xa = xs[:, :, 4], xs[:, :, 5]
    lw = p['rwkv_decay0'][j] + jnp.einsum(
        'bszr,zre->bsze', jnp.tanh(jnp.einsum('bsd,zdr->bszr', xw, p['rwkv_decay1'][j])), p['rwkv_decay2'][j])
    decay = jnp.exp(-jnp.exp(-jax.nn.softplus(-lw.astype(jnp.float32)) - 0.5))
    icl = jax.nn.sigmoid((p['rwkv_icl0'][j] + jnp.einsum(
        'bszr,zre->bsze', jnp.einsum('bsd,zdr->bszr', xa, p['rwkv_icl1'][j]), p['rwkv_icl2'][j])).astype(jnp.float32))

    def heads(t):
        return t.reshape(t.shape[:-1] + (RWKV_HEADS, RWKV_HEAD)).astype(jnp.float32)

    kk = heads(k * p['rwkv_k_k'][j])
    kk = kk / jnp.maximum(jnp.sqrt(jnp.sum(kk * kk, axis=-1, keepdims=True)), 1e-12)
    k_dir = k[:, :, None].astype(jnp.float32) * (1.0 + (icl - 1.0) * p['rwkv_k_a'][j].astype(jnp.float32))
    r_h, v_h, k_h, w_h, a_h = heads(r), heads(v), heads(k_dir), heads(decay), heads(icl)

    def two(t):
        return jnp.broadcast_to(t[:, :, None], (b, s, 2) + t.shape[2:])

    y, s_final = bidir_delta_scan(two(r_h), w_h, k_h, two(v_h), two(kk), a_h, s0)
    y = y.sum(axis=2)
    mu = jnp.mean(y, axis=-1, keepdims=True)
    var = jnp.mean(jnp.square(y - mu), axis=-1, keepdims=True)
    y = ((y - mu) * lax.rsqrt(var + GN_EPS)).reshape(b, s, D_INNER)
    y = y * p['rwkv_gn_w'][j].astype(jnp.float32) + p['rwkv_gn_b'][j].astype(jnp.float32)
    bonus = (jnp.sum(r_h[:, :, None] * k_h * p['rwkv_r_k'][j].astype(jnp.float32), axis=-1, keepdims=True)
             * v_h[:, :, None]).sum(axis=2).reshape(b, s, D_INNER)
    out = ((y + bonus) * jax.nn.silu(g.astype(jnp.float32))).astype(h.dtype)
    return out @ p['rwkv_w_out'][j], s_final.astype(h.dtype)

def attn_qkvg(h, p, j):
    b, s, _ = h.shape
    nq, nk = N_HEADS * HEAD_DIM, KV_HEADS * HEAD_DIM
    proj = h @ p['attn_w_in'][j]
    q = rmsnorm(proj[..., :nq].reshape(b, s, N_HEADS, HEAD_DIM), p['attn_q_norm'][j])
    k = rmsnorm(proj[..., nq:nq + nk].reshape(b, s, KV_HEADS, HEAD_DIM), p['attn_k_norm'][j])
    v = proj[..., nq + nk:nq + 2 * nk].reshape(b, s, KV_HEADS, HEAD_DIM)
    g = proj[..., nq + 2 * nk:]
    return q, k, v, g

def attn_context(h, p, j):
    q, k, v, g = attn_qkvg(h, p, j)
    o = block_attention(q, k, v)
    return (o * jax.nn.silu(g)) @ p['attn_w_out'][j], (k, v)

def attn_latent(h, p, j, k_ctx, v_ctx, cos, sin):
    q, k, v, g = attn_qkvg(h, p, j)
    q, k = rope2d(q, cos, sin), rope2d(k, cos, sin)
    k_all = jnp.concatenate([k, k_ctx.astype(k.dtype)], axis=1)
    v_all = jnp.concatenate([v, v_ctx.astype(v.dtype)], axis=1)
    o = block_attention(q, k_all, v_all)
    return (o * jax.nn.silu(g)) @ p['attn_w_out'][j]

def conv_mixer(h, p, j):
    proj = h @ p['conv_w_in'][j]
    bg, cg, u, g = jnp.split(proj, 4, axis=-1)
    u = cg * u
    prev, nxt = neighbours(u)
    w = p['conv_w'][j]
    u = prev * w[0] + u * w[1] + nxt * w[2] + p['conv_b'][j]
    return (bg * u * jax.nn.silu(g)) @ p['conv_w_out'][j]

def sublayer(x, cond, p, i, mixer_fn):
    ada = jax.nn.silu(cond) @ p['w_ada'][i] + p['b_ada'][i]
    shift, scale, gate = jnp.split(ada[:, None, :], 3, axis=-1)
    h = rmsnorm(x, p['norm_pre'][i]) * (1.0 + scale) + shift
    m, extra = mixer_fn(h)
    return x + gate * rmsnorm(m, p['norm_post'][i]), extra

def setup_inputs(seed: int = 0) -> dict:
    key = jax.random.key(seed)
    ks = iter(jax.random.split(key, 64))
    D, E = D_MODEL, D_INNER

    def nrm(shape, scale):
        return jax.random.normal(next(ks), shape, jnp.float32) * scale

    def uni(shape):
        return jax.random.uniform(next(ks), shape, jnp.float32)

    return {
        'x_prompt': nrm((BATCH, SEQ, D), 1.0),
        'x_sample': nrm((DEC_BATCH, DEC_SEQ, D), 1.0),
        'state_rwkv': nrm((DEC_BATCH, N_LAYERS_A, 2, RWKV_HEADS, RWKV_HEAD, RWKV_HEAD), 0.3),
        'cache_k': nrm((DEC_BATCH, N_LAYERS_B, PAST_LEN, KV_HEADS, HEAD_DIM), 1.0),
        'cache_v': nrm((DEC_BATCH, N_LAYERS_B, PAST_LEN, KV_HEADS, HEAD_DIM), 1.0),
        'c': nrm((DEC_BATCH, D), 1.0),
        'c_ctx': nrm((D,), 1.0),
        'norm_pre': 1.0 + nrm((DEPTH, D), 0.02),
        'norm_post': 1.0 + nrm((DEPTH, D), 0.02),
        'w_ada': nrm((DEPTH, D, 3 * D), 0.5 * D ** -0.5),
        'b_ada': nrm((DEPTH, 3 * D), 0.02),
        'rwkv_mu': uni((N_LAYERS_A, 6, D)),
        'rwkv_w_in': nrm((N_LAYERS_A, 4, D, E), D ** -0.5),
        'rwkv_decay0': nrm((N_LAYERS_A, 2, E), 0.5),
        'rwkv_decay1': nrm((N_LAYERS_A, 2, D, DECAY_LORA), D ** -0.5),
        'rwkv_decay2': nrm((N_LAYERS_A, 2, DECAY_LORA, E), 0.3 * DECAY_LORA ** -0.5),
        'rwkv_icl0': nrm((N_LAYERS_A, 2, E), 0.5),
        'rwkv_icl1': nrm((N_LAYERS_A, 2, D, ICL_LORA), D ** -0.5),
        'rwkv_icl2': nrm((N_LAYERS_A, 2, ICL_LORA, E), 0.3 * ICL_LORA ** -0.5),
        'rwkv_k_k': 0.85 + nrm((N_LAYERS_A, E), 0.02),
        'rwkv_k_a': 1.0 + nrm((N_LAYERS_A, E), 0.02),
        'rwkv_r_k': nrm((N_LAYERS_A, RWKV_HEADS, RWKV_HEAD), 0.1),
        'rwkv_gn_w': 1.0 + nrm((N_LAYERS_A, E), 0.02),
        'rwkv_gn_b': nrm((N_LAYERS_A, E), 0.02),
        'rwkv_w_out': nrm((N_LAYERS_A, E, D), E ** -0.5),
        'attn_w_in': nrm((N_LAYERS_B, D, ATTN_IN_COLS), D ** -0.5),
        'attn_q_norm': 1.0 + nrm((N_LAYERS_B, HEAD_DIM), 0.02),
        'attn_k_norm': 1.0 + nrm((N_LAYERS_B, HEAD_DIM), 0.02),
        'attn_w_out': nrm((N_LAYERS_B, E, D), E ** -0.5),
        'conv_w_in': nrm((N_LAYERS_C, D, 4 * E), D ** -0.5),
        'conv_w': nrm((N_LAYERS_C, CONV_W, E), CONV_W ** -0.5),
        'conv_b': nrm((N_LAYERS_C, E), 0.02),
        'conv_w_out': nrm((N_LAYERS_C, E, D), E ** -0.5),
    }

def reference(x_prompt, x_sample, state_rwkv, cache_k, cache_v, c, c_ctx,
              norm_pre, norm_post, w_ada, b_ada,
              rwkv_mu, rwkv_w_in, rwkv_decay0, rwkv_decay1, rwkv_decay2,
              rwkv_icl0, rwkv_icl1, rwkv_icl2, rwkv_k_k, rwkv_k_a, rwkv_r_k,
              rwkv_gn_w, rwkv_gn_b, rwkv_w_out,
              attn_w_in, attn_q_norm, attn_k_norm, attn_w_out,
              conv_w_in, conv_w, conv_b, conv_w_out):
    p = dict(norm_pre=norm_pre, norm_post=norm_post, w_ada=w_ada, b_ada=b_ada,
             rwkv_mu=rwkv_mu, rwkv_w_in=rwkv_w_in, rwkv_decay0=rwkv_decay0,
             rwkv_decay1=rwkv_decay1, rwkv_decay2=rwkv_decay2, rwkv_icl0=rwkv_icl0,
             rwkv_icl1=rwkv_icl1, rwkv_icl2=rwkv_icl2, rwkv_k_k=rwkv_k_k, rwkv_k_a=rwkv_k_a,
             rwkv_r_k=rwkv_r_k, rwkv_gn_w=rwkv_gn_w, rwkv_gn_b=rwkv_gn_b, rwkv_w_out=rwkv_w_out,
             attn_w_in=attn_w_in, attn_q_norm=attn_q_norm, attn_k_norm=attn_k_norm,
             attn_w_out=attn_w_out, conv_w_in=conv_w_in, conv_w=conv_w, conv_b=conv_b,
             conv_w_out=conv_w_out)

    x = x_prompt
    cond_ctx = c_ctx[None, :]
    new_s, new_k, new_v = [], [], []
    for i in range(DEPTH):
        j, kind = i // N_MIXERS, i % N_MIXERS
        if kind == 0:
            s0 = jnp.zeros((x.shape[0], 2, RWKV_HEADS, RWKV_HEAD, RWKV_HEAD), jnp.float32)
            x, st = sublayer(x, cond_ctx, p, i, lambda h: rwkv_mixer(h, p, j, s0))
            new_s.append(st)
        elif kind == 1:
            x, kv = sublayer(x, cond_ctx, p, i, lambda h: attn_context(h, p, j))
            new_k.append(kv[0])
            new_v.append(kv[1])
        else:
            x, _ = sublayer(x, cond_ctx, p, i, lambda h: (conv_mixer(h, p, j), None))
    y_prompt = x

    rows = x_sample.shape[1] // GRID_W
    cos, sin = axial_rope_tables(rows)
    x = x_sample
    for i in range(DEPTH):
        j, kind = i // N_MIXERS, i % N_MIXERS
        if kind == 0:
            s0 = state_rwkv[:, j].astype(jnp.float32)
            x, _ = sublayer(x, c, p, i, lambda h: rwkv_mixer(h, p, j, s0))
        elif kind == 1:
            x, _ = sublayer(x, c, p, i, lambda h: (attn_latent(h, p, j, cache_k[:, j], cache_v[:, j], cos, sin), None))
        else:
            x, _ = sublayer(x, c, p, i, lambda h: (conv_mixer(h, p, j), None))
    y_sample = x

    return (y_prompt, y_sample, jnp.stack(new_s, axis=1), jnp.stack(new_k, axis=1), jnp.stack(new_v, axis=1))


_drawn_inputs = setup_inputs


def setup_inputs(seed=0):
    import zlib

    import numpy as np

    out = dict(_drawn_inputs(seed))
    spreads = {}
    factors = {'state_rwkv': 5.022,
     'cache_k': 3.099,
     'norm_post': 4.363,
     'rwkv_k_k': 5.922,
     'rwkv_gn_w': 6.891,
     'rwkv_gn_b': 6.189,
     'attn_q_norm': 8.0,
     'attn_k_norm': 2.685,
     'conv_b': 8.0}
    for name, (base, spread) in spreads.items():
        noise = np.random.default_rng([zlib.crc32(name.encode()), seed]).standard_normal(out[name].shape)
        drawn = base * np.exp(spread * noise) if base else spread * noise
        out[name] = __import__('jax').numpy.asarray(drawn.astype(out[name].dtype))
    for name, factor in factors.items():
        out[name] = (out[name] * factor).astype(out[name].dtype)
    return out
```

```python
from contextlib import ExitStack
import math

import numpy as np

import concourse.bass as bass
from concourse import mybir
from concourse.alu_op_type import AluOpType as ALU

ACT = mybir.ActivationFunctionType
F32 = mybir.dt.float32

P = 128
D = 1024
NB = D // P
CTX = 128
LAT = 1024
T = CTX + LAT
NT = T // P
NLT = LAT // P
CH = 3
CW = T // CH
HD = 64
RMS_EPS = 1e-6
GN_EPS = 64e-5
DECAY_SCALE = math.exp(-0.5)
LEVELS = 7
WSLOTS = 2

MIXER = (0, 1, 2, 0)

A_SW0, A_A0, A_R, A_K, A_KK, A_V, A_SW1, A_A1, A_G = range(9)
R_SW, R_A, R_R, R_K, R_KK, R_V = range(6)


class Core:
    pass


def build(nc, io, layers=(0, 1, 2, 3)):
    g = Core()
    g.io = io
    dram = lambda name, shape: nc.dram_tensor(name, shape, F32, kind="Internal").ap()
    g.scan_in = dram("scan_in", (NT * NB, 9, P, P))
    g.scan_y = dram("scan_y", (NT * NB, P, 2, P))
    g.state = dram("state_chain", ((NT + 1) * NB, P, 2, HD))

    ctx = ExitStack()
    with ctx:
        sb = lambda name, shape: ctx.enter_context(nc.sbuf_tensor(name, shape, F32))
        g.x = sb("x_resid", [P, NB, T])
        g.slab = sb("w_slab", [P, WSLOTS, NB * P])
        g.arena = sb("arena", [P, 4 * NB * T])
        g.stage = sb("stage", [P, 2, T])
        g.ones = sb("ones", [P, P])
        g.ident = sb("ident", [P, P])
        g.extra = sb("extra", [P, T + P])
        g.eps = sb("eps", [P, 1])
        g.flag = sb("flag", [P, 4])
        g.head_ones = sb("head_ones", [P, P])
        g.ada = sb("ada", [P, 4, 24, 2])
        g.chan = sb("chan", [P, io["chan"].shape[1]])
        g.ps = ctx.enter_context(nc.psum_tensor("ps", [P, 8, 512], F32))
        n = NB * T
        g.big = [g.arena[:, i * n:(i + 1) * n].rearrange("p (b t) -> p b t", b=NB) for i in range(4)]

        phase_start(nc, g)
        for layer in layers:
            j = layer // 3
            phase_prenorm(nc, g, layer)
            if MIXER[layer] == 0:
                phase_rwkv_project(nc, g, layer, j)
                phase_rwkv_lora(nc, g, j)
                phase_scan(nc, g, j)
                phase_rwkv_finish(nc, g, j)
            elif MIXER[layer] == 1:
                phase_attention_project(nc, g)
                phase_attention(nc, g)
            else:
                phase_conv(nc, g)
            phase_output(nc, g, layer)
        phase_end(nc, g)


CHAN = {}


def chan_layout():
    if CHAN:
        return CHAN
    at = 0
    for name, n in (("norm_pre", 32), ("norm_post", 32), ("b_ada", 96), ("mu", 96), ("decay0", 32), ("icl0", 32),
                    ("k_k", 16), ("r_k", 16), ("gn_w", 16), ("gn_b", 16), ("k_a", 16), ("q_norm", 1), ("k_norm", 1),
                    ("conv_w", 24), ("conv_b", 8)):
        CHAN[name] = at
        at += n
    CHAN["_"] = at
    return CHAN


def ch(g, name, i, n=1):
    at = chan_layout()[name] + i
    return g.chan[:, at:at + n]


def slot_view(ps_banks):
    return ps_banks[:, :, 0:CW]


def as3(ap):
    return ap.rearrange("p (c n) -> p c n", c=CH)


class Sems:

    def __init__(self, nc, ctx):
        self.nc, self.taken = nc, []
        Sems.phases += 1
        ctx.callback(self.release)

    phases = 0

    def release(self):
        self.nc.clear_and_free_semaphores(self.taken)
        self.nc.all_engine_barrier()

    def __call__(self, *names):
        got = [self.nc.alloc_semaphore(f"{n}_{Sems.phases}") for n in names]
        self.taken += got
        return got[0] if len(got) == 1 else got


def phase_start(nc, g):
    io = g.io
    c = chan_layout()
    with ExitStack() as ctx:
        sem = Sems(nc, ctx)
        loaded, ident_in, cond_ok, sig_ok, silu_ok, rows_mm, rows_sb, cols_mm, cols_sb, vec_ok, set_ok = sem(
            "loaded", "ident_in", "cond_in", "sig_ok", "silu_ok", "rows_mm", "rows_sb", "cols_mm", "cols_sb", "vec_ok", "set_ok")
        wa_in = [sem(f"wa_in{i}") for i in range(2)]
        wsz = NB * 512
        wa = [g.arena[:, i * wsz:(i + 1) * wsz].rearrange("p (k n) -> p k n", k=NB) for i in range(2)]
        at = 2 * wsz
        rows = g.arena[0:2, at:at + 3072]
        at += 3072
        cond = g.arena[:, at:at + 16].rearrange("p (k c) -> p k c", c=2)
        sig = g.arena[:, at + 16:at + 32].rearrange("p (k c) -> p k c", c=2)
        silu = g.arena[:, at + 32:at + 48].rearrange("p (k c) -> p k c", c=2)
        block = ctx.enter_context(nc.Block())

        @block.sync
        def _(sp):
            sp.dma_start(cond, io["cond"]).then_inc(cond_ok, 16)
            sp.dma_start(g.ident[:, :], io["ident"]).then_inc(ident_in, 16)
            sp.dma_start(g.chan[:, :], io["chan"]).then_inc(loaded, 16)
            sp.dma_start(g.x[:, :, :], io["x"]).then_inc(loaded, 16)
            sp.dma_start(g.ones[:, :], io["ones"]).then_inc(loaded, 16)
            sp.dma_start(g.head_ones[:, :], io["head_ones"]).then_inc(loaded, 16)
            with sp.Fori(0, 12) as i:
                for s in range(2):
                    sp.wait_ge(rows_mm, 2 * i)
                    sp.dma_start(wa[s], io["w_ada"][bass.ds(2 * i + s, 1)].rearrange("o p k n -> (o p) k n")).then_inc(wa_in[s], 16)
            sp.wait_ge(loaded, 64)

        @block.scalar
        def _(act):
            act.wait_ge(cond_ok, 16)
            nc.scalar.activation(sig, cond, ACT.Sigmoid).then_inc(sig_ok, 1)
            for layer in range(4):
                for q in range(6):
                    act.wait_ge(rows_mm, 6 * layer + q + 1)
                    if q == 0 and layer:
                        act.wait_ge(cols_mm, layer)
                    nc.scalar.copy(rows[:, q * 512:(q + 1) * 512], g.ps[0:2, q % 2, :]).then_inc(rows_sb, 1)

        @block.tensor
        def _(pe):
            pe.wait_ge(silu_ok, 1)
            pe.wait_ge(ident_in, 16)
            for layer in range(4):
                for q in range(6):
                    n = 6 * layer + q
                    pe.wait_ge(wa_in[n % 2], 16 * (n // 2 + 1))
                    if n >= 2:
                        pe.wait_ge(rows_sb, n - 1)
                    for k in range(NB):
                        mm = pe.matmul(g.ps[0:2, n % 2, :], silu[:, k, :], wa[n % 2][:, k, :], start=k == 0, stop=k == NB - 1)
                    mm.then_inc(rows_mm, 1)
                pe.wait_ge(rows_sb, 6 * layer + 6)
                if layer:
                    pe.wait_ge(cols_sb, layer)
                for b in range(24):
                    mm = pe.transpose(g.ps[:, 2, 2 * b:2 * b + 2], rows[:, b * P:(b + 1) * P], g.ident[0:2, 0:2])
                mm.then_inc(cols_mm, 1)

        @block.vector
        def _(dve):
            nc.vector.memset(g.eps[:, :], GN_EPS).then_inc(set_ok, 1)
            nc.vector.memset(g.flag[:, :], 0.0).then_inc(set_ok, 1)
            dve.wait_ge(set_ok, 2)
            dve.wait_ge(sig_ok, 1)
            nc.vector.tensor_tensor(silu, cond, sig, op=ALU.mult).then_inc(silu_ok, 1)
            dve.wait_ge(loaded, 64)
            k = 0
            for layer in range(4):
                a = g.ada[:, layer]
                dve.wait_ge(cols_mm, layer + 1)
                b0 = c["b_ada"] + 24 * layer
                bias = g.chan[:, b0:b0 + 24].rearrange("p (n o) -> p n o", o=1).to_broadcast([P, 24, 2])
                nc.vector.tensor_tensor(a, g.ps[:, 2, 0:48].rearrange("p (n c) -> p n c", c=2), bias, op=ALU.add).then_inc(cols_sb, 1)
                dve.wait_ge(cols_sb, layer + 1)
                n0 = c["norm_pre"] + 8 * layer
                pre = g.chan[:, n0:n0 + 8].rearrange("p (n o) -> p n o", o=1).to_broadcast([P, 8, 2])
                n1 = c["norm_post"] + 8 * layer
                post = g.chan[:, n1:n1 + 8].rearrange("p (n o) -> p n o", o=1).to_broadcast([P, 8, 2])
                nc.vector.scalar_tensor_tensor(a[:, 8:16, :], a[:, 8:16, :], 1.0, pre, op0=ALU.add, op1=ALU.mult).then_inc(vec_ok, 1)
                nc.vector.tensor_tensor(a[:, 16:24, :], a[:, 16:24, :], post, op=ALU.mult).then_inc(vec_ok, 1)
                k += 2
            dve.wait_ge(vec_ok, k)


def token_ranges():
    return ((0, 0, CTX), (1, CTX, T))


def norm_matmuls(pe, g, sq, sq_ok, used, banks):
    for b in range(NB):
        pe.wait_ge(sq_ok, b + 1)
        for c in range(CH):
            mm = pe.matmul(g.ps[:, banks + c, 0:CW], g.ones[:, :], sq[b % 2][:, c * CW:(c + 1) * CW],
                           start=b == 0, stop=b == NB - 1)
        mm.then_inc(used, 1)


def phase_prenorm(nc, g, layer):
    h = g.big[0]
    tmp = g.big[1]
    sq = [g.big[2][:, i, :] for i in range(2)]
    ms, root, rstd = g.big[2][:, 2, :], g.big[2][:, 3, :], g.big[2][:, 4, :]
    ada = g.ada[:, layer]
    with ExitStack() as ctx:
        sem = Sems(nc, ctx)
        sq_ok, sq_used, ms_ok, root_ok, rstd_ok, tmp_ok, h_ok = sem("sq_ok", "sq_used", "ms_ok", "root_ok", "rstd_ok", "tmp_ok", "h_ok")
        block = ctx.enter_context(nc.Block())

        @block.scalar
        def _(act):
            for b in range(NB):
                if b >= 2:
                    act.wait_ge(sq_used, b - 1)
                nc.scalar.activation(sq[b % 2], g.x[:, b, :], ACT.Square).then_inc(sq_ok, 1)
            act.wait_ge(ms_ok, 1)
            nc.scalar.activation(root, ms, ACT.Sqrt).then_inc(root_ok, 1)
            for b in range(NB):
                act.wait_ge(tmp_ok, b + 1)
                for c, a0, a1 in token_ranges():
                    nc.scalar.activation(h[:, b, a0:a1], tmp[:, b, a0:a1], ACT.Identity, bias=ada[:, b, c:c + 1],
                                         scale=ada[:, 8 + b, c:c + 1]).then_inc(h_ok, 1)
            act.wait_ge(h_ok, 2 * NB)

        @block.tensor
        def _(pe):
            norm_matmuls(pe, g, sq, sq_ok, sq_used, 0)

        @block.vector
        def _(dve):
            dve.wait_ge(sq_used, NB)
            nc.vector.tensor_scalar(as3(ms), slot_view(g.ps[:, 0:3, :]), 1.0 / D, RMS_EPS, ALU.mult, ALU.add).then_inc(ms_ok, 1)
            dve.wait_ge(root_ok, 1)
            nc.vector.reciprocal(rstd, root).then_inc(rstd_ok, 1)
            dve.wait_ge(rstd_ok, 1)
            for b in range(NB):
                nc.vector.tensor_tensor(tmp[:, b, :], g.x[:, b, :], rstd, op=ALU.mult).then_inc(tmp_ok, 1)
            dve.wait_ge(tmp_ok, NB)


def load_slabs(sp, g, first, count, slab_in, proj_done, n0=0):
    def one(n, s, free=True):
        if free:
            sp.wait_ge(proj_done, n - WSLOTS + 1)
        src = g.io["w"][bass.ds(first - n0 + n, 1)].rearrange("o p k -> (o p) k")
        sp.dma_start(g.slab[:, s, :], src).then_inc(slab_in[s], 16)

    n = n0
    end = n0 + count
    while n < end and n < WSLOTS:
        one(n, n % WSLOTS, free=False)
        n += 1
    groups = (end - n) // WSLOTS
    if groups > 1:
        with sp.Fori(0, groups) as i:
            for u in range(WSLOTS):
                one(n + u + WSLOTS * i, (n + u) % WSLOTS)
        n += WSLOTS * groups
    while n < end:
        one(n, n % WSLOTS)
        n += 1


def multiply(pe, g, rhs, slot, bank, done):
    for k in range(NB):
        for c in range(CH):
            mm = pe.matmul(g.ps[:, bank + c, 0:CW], g.slab[:, slot, k * P:(k + 1) * P], rhs[:, k, c * CW:(c + 1) * CW],
                           start=k == 0, stop=k == NB - 1)
    mm.then_inc(done, 1)


def project(pe, g, rhs, count, n0, slab_in, evacuated, proj_done):
    def one(n, u):
        s = (n0 + u) % WSLOTS
        bank = 3 * ((n0 + u) % 2)
        pe.wait_ge(slab_in[s], 16 * (n // WSLOTS + 1) if isinstance(n, int) else (n - s) * (16 // WSLOTS) + 16)
        if not isinstance(n, int) or n >= 2:
            pe.wait_ge(evacuated, n - 1)
        multiply(pe, g, rhs, s, bank, proj_done)

    if count % WSLOTS == 0 and count > WSLOTS and n0 >= 0:
        start = 0
        if n0 < 2:
            for u in range(WSLOTS):
                one(n0 + u, u)
            start = 1
        if count // WSLOTS - start > 1:
            with pe.Fori(start, count // WSLOTS) as i:
                for u in range(WSLOTS):
                    one(n0 + u + WSLOTS * i, u)
        else:
            for u in range(WSLOTS * start, count):
                one(n0 + u, u)
    else:
        for u in range(count):
            one(n0 + u, u)


W_RWKV = 34


def w_base(name, j=0):
    if name == "rwkv":
        return j * (W_RWKV + NB)
    at = 2 * (W_RWKV + NB)
    if name == "attn":
        return at
    at += 18 + NB
    return at


def phase_rwkv_project(nc, g, layer, j):
    h, xx, xs = g.big[0], g.big[1], [g.big[2], g.big[3]]
    lora = [g.big[0][:, 0, :], g.big[0][:, 1, :]]
    base = w_base("rwkv", j)
    with ExitStack() as ctx:
        sem = Sems(nc, ctx)
        half_ok, xx_ok, xs_ok, proj_done, evacuated = sem("half_ok", "xx_ok", "xs_ok", "proj_done", "evacuated")
        slab_in = [sem(f"slab_in{i}") for i in range(WSLOTS)]
        stored = [sem(f"stored{i}") for i in range(2)]
        block = ctx.enter_context(nc.Block())
        ranges = token_ranges()

        @block.sync
        def _(sp):
            load_slabs(sp, g, base, W_RWKV, slab_in, proj_done)

        @block.tensor
        def _(pe):
            for m in range(4):
                pe.wait_ge(xs_ok, NB * (m + 1))
                project(pe, g, xs[m % 2], NB, NB * m, slab_in, evacuated, proj_done)
            for m in (4, 5):
                pe.wait_ge(xs_ok, NB * (m + 1))
                project(pe, g, xs[m % 2], 1, 32 + m - 4, slab_in, evacuated, proj_done)

        @block.scalar
        def _(act):
            for m in range(4):
                arr = (A_R, A_K, A_V, A_G)[m]
                for b in range(NB):
                    n = NB * m + b
                    act.wait_ge(proj_done, n + 1)
                    if n >= 2:
                        act.wait_ge(stored[n % 2], 16 * (n // 2))
                    st = g.stage[:, n % 2, :]
                    nc.scalar.copy(as3(st), slot_view(g.ps[:, 3 * (n % 2):3 * (n % 2) + 3, :])).then_inc(evacuated, 1)
                    act.wait_ge(evacuated, n + 1)
                    dst = g.scan_in[b::NB, arr].rearrange("t p n -> p t n")
                    act.dma_start(dst, st.rearrange("p (t n) -> p t n", n=P)).then_inc(stored[n % 2], 16)
            act.wait_ge(xs_ok, 6 * NB)
            for m in (4, 5):
                n = 32 + m - 4
                act.wait_ge(proj_done, n + 1)
                fn = ACT.Tanh if m == 4 else ACT.Copy
                nc.scalar.activation(as3(lora[m - 4]), slot_view(g.ps[:, 3 * (n % 2):3 * (n % 2) + 3, :]), fn).then_inc(evacuated, 1)
            act.wait_ge(evacuated, 34)
            for s in range(2):
                act.wait_ge(stored[s], 16 * 16)

        @block.vector
        def _(dve):
            for b in range(NB):
                for _, a0, a1 in ranges:
                    nc.vector.tensor_tensor(xx[:, b, a0 + 1:a1 - 1], h[:, b, a0:a1 - 2], h[:, b, a0 + 2:a1], op=ALU.add).then_inc(half_ok, 1)
                    nc.vector.tensor_copy(xx[:, b, a0:a0 + 1], h[:, b, a0 + 1:a0 + 2]).then_inc(half_ok, 1)
                    nc.vector.tensor_copy(xx[:, b, a1 - 1:a1], h[:, b, a1 - 2:a1 - 1]).then_inc(half_ok, 1)
            for b in range(NB):
                dve.wait_ge(half_ok, 6 * (b + 1))
                nc.vector.scalar_tensor_tensor(xx[:, b, :], xx[:, b, :], 0.5, h[:, b, :], op0=ALU.mult, op1=ALU.subtract).then_inc(xx_ok, 1)
            for m in range(6):
                if m >= 2:
                    dve.wait_ge(proj_done, NB * (m - 1))
                for b in range(NB):
                    if m == 0:
                        dve.wait_ge(xx_ok, b + 1)
                    mu = ch(g, "mu", 48 * j + 8 * m + b)
                    nc.vector.scalar_tensor_tensor(xs[m % 2][:, b, :], xx[:, b, :], mu, h[:, b, :], op0=ALU.mult, op1=ALU.add).then_inc(xs_ok, 1)
            dve.wait_ge(xs_ok, 6 * NB)


def phase_rwkv_lora(nc, g, j):
    lora = [g.big[0][:, 0, :], g.big[0][:, 1, :]]
    up = g.big[1][:, 0:4, :].rearrange("p b t -> p (b t)")[:, 0:2 * 16 * P].rearrange("p (m n) -> p m n", n=P)
    keys = [g.big[2][:, i, :] for i in range(2)]
    kc = [g.big[2][:, 2 + i, :] for i in range(2)]
    sq = [g.big[2][:, 4 + i, :] for i in range(2)]
    root = [g.big[2][:, 6 + i, :] for i in range(2)]
    inv = [g.big[3][:, i, :] for i in range(2)]
    with ExitStack() as ctx:
        sem = Sems(nc, ctx)
        up_in, up_mm, up_sb, kc_ok, sq_ok, norm_mm, root_ok, clamp_ok, inv_ok, kk_ok = sem(
            "up_in", "up_mm", "up_sb", "kc_ok", "sq_ok", "norm_mm", "root_ok", "clamp_ok", "inv_ok", "kk_ok")
        key_in = [sem(f"key_in{i}") for i in range(2)]
        stored = [sem(f"stored{i}") for i in range(2)]
        kk_stored = [sem(f"kk_stored{i}") for i in range(2)]
        block = ctx.enter_context(nc.Block())

        @block.sync
        def _(sp):
            sp.dma_start(up, g.io["lora_up"][j]).then_inc(up_in, 16)
            for b in range(NB):
                if b >= 2:
                    sp.wait_ge(kc_ok, b - 1)
                sp.dma_start(keys[b % 2].rearrange("p (t n) -> p t n", n=P),
                             g.scan_in[b::NB, A_K].rearrange("t p n -> p t n")).then_inc(key_in[b % 2], 16)
                if b >= 1:
                    q = b - 1
                    sp.wait_ge(kk_ok, q + 1)
                    sp.dma_start(g.scan_in[q::NB, A_KK].rearrange("t p n -> p t n"),
                                 inv[q % 2].rearrange("p (t n) -> p t n", n=P)).then_inc(kk_stored[q % 2], 16)
            q = NB - 1
            sp.wait_ge(kk_ok, q + 1)
            sp.dma_start(g.scan_in[q::NB, A_KK].rearrange("t p n -> p t n"),
                         inv[q % 2].rearrange("p (t n) -> p t n", n=P)).then_inc(kk_stored[q % 2], 16)
            for s in range(2):
                sp.wait_ge(kk_stored[s], 64)

        @block.tensor
        def _(pe):
            pe.wait_ge(up_in, 16)

            def rates(b):
                for z in range(2):
                    for w in range(2):
                        n = 4 * b + 2 * z + w
                        if n:
                            pe.wait_ge(up_sb, n)
                        for c in range(CH):
                            mm = pe.matmul(g.ps[:, c, 0:CW], up[:, (w * 2 + z) * NB + b, :], lora[w][:, c * CW:(c + 1) * CW],
                                           start=True, stop=True)
                        mm.then_inc(up_mm, 1)

            for b in range(NB):
                rates(b)
                pe.wait_ge(sq_ok, b + 1)
                if b:
                    pe.wait_ge(root_ok, b)
                for c in range(CH):
                    mm = pe.matmul(g.ps[:, 3 + c, 0:CW], g.head_ones[:, :], sq[b % 2][:, c * CW:(c + 1) * CW], start=True, stop=True)
                mm.then_inc(norm_mm, 1)

        @block.scalar
        def _(act):
            for b in range(NB):
                for z in range(2):
                    for w in range(2):
                        n = 4 * b + 2 * z + w
                        act.wait_ge(up_mm, n + 1)
                        if n >= 2:
                            act.wait_ge(stored[n % 2], 16 * (n // 2))
                        st = g.stage[:, n % 2, :]
                        bias = ch(g, "icl0" if w else "decay0", 16 * j + 8 * z + b)
                        nc.scalar.activation(as3(st), slot_view(g.ps[:, 0:3, :]), ACT.Sigmoid, bias=bias).then_inc(up_sb, 1)
                        act.wait_ge(up_sb, n + 1)
                        arr = ((A_SW0, A_A0), (A_SW1, A_A1))[z][w]
                        act.dma_start(g.scan_in[b::NB, arr].rearrange("t p n -> p t n"),
                                      st.rearrange("p (t n) -> p t n", n=P)).then_inc(stored[n % 2], 16)
                act.wait_ge(norm_mm, b + 1)
                if b >= 2:
                    act.wait_ge(clamp_ok, b - 1)
                    act.wait_ge(inv_ok, b - 1)
                nc.scalar.activation(as3(root[b % 2]), slot_view(g.ps[:, 3:6, :]), ACT.Sqrt).then_inc(root_ok, 1)
            for s in range(2):
                act.wait_ge(stored[s], 16 * 16)

        @block.vector
        def _(dve):
            def scaled(b):
                dve.wait_ge(key_in[b % 2], 16 * (b // 2 + 1))
                if b >= 2:
                    dve.wait_ge(kk_ok, b - 1)
                nc.vector.tensor_scalar(kc[b % 2], keys[b % 2], ch(g, "k_k", 8 * j + b), None, ALU.mult).then_inc(kc_ok, 1)
                dve.wait_ge(kc_ok, b + 1)
                if b >= 2:
                    dve.wait_ge(norm_mm, b - 1)
                nc.vector.tensor_tensor(sq[b % 2], kc[b % 2], kc[b % 2], op=ALU.mult).then_inc(sq_ok, 1)

            scaled(0)
            for b in range(NB):
                if b + 1 < NB:
                    scaled(b + 1)
                dve.wait_ge(root_ok, b + 1)
                nc.vector.tensor_scalar(root[b % 2], root[b % 2], 1e-12, None, ALU.max).then_inc(clamp_ok, 1)
                dve.wait_ge(clamp_ok, b + 1)
                if b >= 2:
                    dve.wait_ge(kk_stored[b % 2], 16 * (b // 2))
                nc.vector.reciprocal(inv[b % 2], root[b % 2]).then_inc(inv_ok, 1)
                dve.wait_ge(inv_ok, b + 1)
                nc.vector.tensor_tensor(inv[b % 2], inv[b % 2], kc[b % 2], op=ALU.mult).then_inc(kk_ok, 1)


PAIRS = NT * NB // 2
CTX_PAIRS = NB // 2
MASKS = {name: i for i, name in enumerate(("strict", "incl", "lv0", "lv0t", "lv1", "lv2", "lv3", "lv4", "lv5", "lv6", "eye"))}


def phase_scan(nc, g, j):
    io = g.io
    at = [0]

    def take(*shape):
        n = int(np.prod(shape))
        ap = g.arena[:, at[0]:at[0] + n]
        at[0] += n
        assert at[0] <= 4 * NB * T
        names = "abcd"[:len(shape)]
        if len(shape) == 1:
            return ap
        return ap.rearrange("p (%s) -> p %s" % (" ".join(names), " ".join(names)), **dict(zip(names, shape)))

    raw = [take(6, 4, P) for _ in range(2)]
    ka = [take(4) for _ in range(2)]
    wA, wR, wK, wB = [[take(4, P) for _ in range(2)] for _ in range(4)]
    inv_t, tak_t, trb_t, trk_t = [[[take(4, P) for _h in range(2)] for _ in range(2)] for _ in range(4)]
    tokB, tokK, tokV = [[take(4, P) for _ in range(2)] for _ in range(3)]
    tab_t, X, XT, U = [[take(4, P) for _h in range(2)] for _ in range(4)]
    cum, d1, d0, kd, bb, eA, eR, eB = [take(4, P) for _ in range(8)]
    masks = take(len(MASKS), 2, P)
    reset = take(4 * P)
    f_in, f_out = [[take(4) for _ in range(2)] for _ in range(2)]
    rhs_sb_, sa_sb_ = [[take(4, HD) for _h in range(2)] for _ in range(2)]
    hs, hn = take(4, HD), take(4, HD)
    stage = g.stage[:, :, :].rearrange("p a b -> p (a b)")
    ystage = [stage[:, i * 512:(i + 1) * 512].rearrange("p (a b) -> p a b", a=4) for i in range(2)]
    hin = [stage[:, 1024 + i * 256:1280 + i * 256].rearrange("p (a b) -> p a b", a=4) for i in range(2)]
    hout = [stage[:, 1536 + i * 256:1792 + i * 256].rearrange("p (a b) -> p a b", a=4) for i in range(2)]

    def mask(name):
        return masks[:, MASKS[name]].rearrange("p (o d) n -> p o d n", o=1).to_broadcast([P, 2, 2, P])

    def sd(ap):
        return ap.rearrange("p (s d) n -> p s d n", s=2)

    def bank(i):
        return g.ps[:, i, :].rearrange("p (a n) -> p a n", a=4)

    b_u, b_x, b_xt, b_ch = [[bank(2 * i), bank(2 * i + 1)] for i in range(4)]
    ch_rhs = [g.ps[:, 6 + h, 0:256].rearrange("p (a n) -> p a n", a=4) for h in range(2)]
    ch_sa = [g.ps[:, 6 + h, 256:512].rearrange("p (a n) -> p a n", a=4) for h in range(2)]
    rows = [slice(0, HD), slice(HD, P)]
    cols = rows
    V = nc.vector

    with ExitStack() as ctx:
        sem = Sems(nc, ctx)
        const_in, init_in, scan_ok, d1_ok, d0_ok, exp_ok, fac_ok, t_ok, kd_ok, b_ok, w_ok, wp_ok = sem(
            "const_in", "init_in", "scan_ok", "d1_ok", "d0_ok", "exp_ok", "fac_ok", "t_ok", "kd_ok", "b_ok", "w_ok", "wp_ok")
        gram_mm, u_mm, x_mm, late_mm, tok_mm = sem("gram_mm", "u_mm", "x_mm", "late_mm", "tok_mm")
        tab_ok, x0_ok, eye_ok, u_ok, xa_ok, xt_ok, late_ok, tok_ok = sem(
            "tab_ok", "x0_ok", "eye_ok", "u_ok", "xa_ok", "xt_ok", "late_ok", "tok_ok")
        rhs_mm, sa_mm, st_mm, y_mm, rhs_ok, sa_ok, y_ok, hs_ok, hn_ok, ho_ok = sem(
            "rhs_mm", "sa_mm", "st_mm", "y_mm", "rhs_ok", "sa_ok", "y_ok", "hs_ok", "hn_ok", "ho_ok")
        raw_in, hin_in, y_stored, h_stored = [[sem(f"{n}{i}") for i in range(2)] for n in ("raw_in", "hin_in", "y_stored", "h_stored")]
        block = ctx.enter_context(nc.Block())

        def each_pair(eng, fn):
            for q in range(6):
                fn(q, q % 2, q // 2)
            with eng.Fori(3, PAIRS // 2 - 1) as i:
                for p in range(2):
                    fn(2 * i + p, p, i)
            for q in range(PAIRS - 2, PAIRS):
                fn(q, q % 2, q // 2)

        known = lambda q: isinstance(q, int)

        @block.sync
        def _(sp):
            sp.dma_start(masks, io["masks"]).then_inc(const_in, 16)
            sp.dma_start(reset, io["reset"]).then_inc(const_in, 16)
            sp.dma_start(g.state[0:NB], io["state_in"][j]).then_inc(init_in, 16)

            def load_raw(q, p, i):
                for s in range(2):
                    n = 2 * q + s
                    back = (NB - 1 - n) if known(q) and q < CTX_PAIRS else ((NT + 1) * NB - 1) - n
                    f = lambda a0, a1, m: g.scan_in[bass.ds(m, 1), a0:a1].rearrange("o a p t -> p (o a) t")
                    sp.dma_start(raw[p][:, 0:6, 2 * s, :], f(A_SW0, A_V + 1, n)).then_inc(raw_in[p], 16)
                    sp.dma_start(raw[p][:, 2:6, 2 * s + 1, :], f(A_R, A_V + 1, back)).then_inc(raw_in[p], 16)
                    sp.dma_start(raw[p][:, 0:2, 2 * s + 1, :], f(A_SW1, A_A1 + 1, back)).then_inc(raw_in[p], 16)
                sp.dma_start(ka[p], io["ka"][j][bass.ds(q, 1)].rearrange("o p n -> (o p) n")).then_inc(raw_in[p], 16)

            load_raw(0, 0, 0)

            def pair(q, p, i):
                if not known(q) or q + 1 < PAIRS:
                    if not known(q) or q >= 1:
                        sp.wait_ge(tok_mm, 3 * q)
                    sp.wait_ge(init_in, 16)
                    load_raw(q + 1, 1 - p, 0)
                if not known(q) or q >= CTX_PAIRS:
                    sp.wait_ge(hs_ok, 4 * (q - 1))
                    sp.wait_ge(init_in, 16)
                    if not known(q) or q >= 2 * CTX_PAIRS:
                        sp.wait_ge(h_stored[p], 16 * i - 16)
                    sp.wait_ge(init_in, 16)
                    for_slot = 2 * q - NB
                    sp.dma_start(hin[p].rearrange("p (s d) n -> p s d n", s=2),
                                 g.state[bass.ds(for_slot, 2)].rearrange("s p d n -> p s d n")).then_inc(hin_in[p], 16)
            each_pair(sp, pair)

        @block.tensor
        def _(pe):
            def units():
                return range(4)

            def chain_rhs(c, p):
                pe.wait_ge(hs_ok, 4 * c + 4)
                pe.wait_ge(y_ok, 2 * c)
                for h in range(2):
                    for u in units():
                        pe.matmul(ch_rhs[h][:, u, :], wA[p][rows[h], u, :], hs[rows[h], u, :], start=True, stop=False)
                        mm = pe.matmul(ch_rhs[h][:, u, :], tak_t[p][h][:, u, :], tokV[p][:, u, cols[h]], start=False, stop=True)
                    mm.then_inc(rhs_mm, 1)

            def chain_sa(c, p):
                for h in range(2):
                    pe.wait_ge(rhs_ok, 2 * c + h + 1)
                    for u in units():
                        mm = pe.matmul(ch_sa[h][:, u, :], inv_t[p][h][:, u, :], rhs_sb_[h][:, u, :], start=True, stop=True)
                    mm.then_inc(sa_mm, 1)

            def chain_state(c, p):
                for h in range(2):
                    pe.wait_ge(sa_ok, 2 * c + h + 1)
                    for u in units():
                        pe.matmul(ch_rhs[h][rows[h], u, :], tokB[p][:, u, cols[h]], sa_sb_[h][:, u, :], start=True, stop=False)
                        mm = pe.matmul(ch_rhs[h][rows[h], u, :], tokK[p][:, u, cols[h]], tokV[p][:, u, cols[h]], start=False, stop=True)
                    mm.then_inc(st_mm, 1)

            def chain_y(c, p):
                for h in range(2):
                    pe.wait_ge(hn_ok, 2 * c + h + 1)
                    for u in units():
                        out = b_ch[h][rows[h], u, :]
                        pe.matmul(out, sa_sb_[h][:, u, :], trb_t[p][h][:, u, :], start=True, stop=False)
                        pe.matmul(out, hs[rows[h], u, :], wR[p][rows[h], u, :], start=False, stop=False)
                        mm = pe.matmul(out, tokV[p][:, u, cols[h]], trk_t[p][h][:, u, :], start=False, stop=True)
                    mm.then_inc(y_mm, 1)

            def pair(q, p, i):
                chain = not known(q) or q >= 1
                c = q - 1
                pe.wait_ge(w_ok, 2 * q + 2)
                pe.wait_ge(wp_ok, 2 * q + 2)
                if chain:
                    pe.wait_ge(tok_ok, 3 * q)
                    pe.wait_ge(late_ok, 6 * q)
                for h in range(2):
                    for u in units():
                        mm = pe.matmul(b_u[h][:, u, :], wB[p][rows[h], u, :], wA[p][rows[h], u, :], start=True, stop=True)
                    mm.then_inc(gram_mm, 1)
                for h in range(2):
                    for u in units():
                        mm = pe.matmul(b_x[h][:, u, :], wA[p][rows[h], u, :], wB[p][rows[h], u, :], start=True, stop=True)
                    mm.then_inc(gram_mm, 1)
                for k in range(1, LEVELS):
                    for h in range(2):
                        if k == 1:
                            pe.wait_ge(tab_ok, 2 * q + h + 1)
                            pe.wait_ge(eye_ok, 4 * q + 2 * h + 2)
                        else:
                            pe.wait_ge(xa_ok, 10 * q + 2 * (k - 2) + h + 1)
                            pe.wait_ge(xt_ok, 12 * q + 2 * (k - 2) + h + 1)
                        for u in units():
                            mm = pe.matmul(b_u[h][:, u, :], tab_t[h][:, u, :], X[h][:, u, :], start=True, stop=True)
                        mm.then_inc(u_mm, 1)
                    if chain:
                        {1: chain_rhs, 2: chain_sa, 3: chain_state, 4: chain_y}.get(k, lambda c, p: None)(c, 1 - p)
                    for h in range(2):
                        pe.wait_ge(u_ok, 12 * q + 2 * (k - 1) + h + 1)
                        if k < LEVELS - 1:
                            for u in units():
                                pe.matmul(b_x[h][:, u, :], XT[h][:, u, :], U[h][:, u, :], start=True, stop=True)
                        for u in units():
                            mm = pe.matmul(b_xt[h][:, u, :], U[h][:, u, :], XT[h][:, u, :], start=True, stop=True)
                        mm.then_inc(x_mm, 1)
                for h in range(2):
                    for u in units():
                        mm = pe.matmul(b_u[h][:, u, :], wK[p][rows[h], u, :], wA[p][rows[h], u, :], start=True, stop=True)
                    mm.then_inc(late_mm, 1)
                for h in range(2):
                    for u in units():
                        mm = pe.matmul(b_x[h][:, u, :], wB[p][rows[h], u, :], wR[p][rows[h], u, :], start=True, stop=True)
                    mm.then_inc(late_mm, 1)
                for h in range(2):
                    pe.wait_ge(xt_ok, 12 * q + 10 + h + 1)
                    for u in units():
                        mm = pe.matmul(b_xt[h][:, u, :], wK[p][rows[h], u, :], wR[p][rows[h], u, :], start=True, stop=True)
                    mm.then_inc(late_mm, 1)
                for t, (bk, src) in enumerate(((b_u[0], wB[p]), (b_u[1], wK[p]), (b_x[0], raw[p][:, R_V]))):
                    pe.wait_ge(late_ok, 6 * q + t + 1)
                    for u in units():
                        mm = pe.transpose(bk[:, u, :], src[:, u, :], g.ident[:, :])
                    mm.then_inc(tok_mm, 1)

            pe.wait_ge(const_in, 32)
            each_pair(pe, pair)
            c, p = PAIRS - 1, 1
            pe.wait_ge(tok_ok, 3 * PAIRS)
            pe.wait_ge(late_ok, 6 * PAIRS)
            chain_rhs(c, p)
            chain_sa(c, p)
            chain_state(c, p)
            chain_y(c, p)

        @block.scalar
        def _(act):
            A = nc.scalar

            def chain_rhs(c):
                for h in range(2):
                    act.wait_ge(rhs_mm, 2 * c + h + 1)
                    A.copy(rhs_sb_[h], ch_rhs[h]).then_inc(rhs_ok, 1)

            def chain_sa(c):
                for h in range(2):
                    act.wait_ge(sa_mm, 2 * c + h + 1)
                    act.wait_ge(y_mm, 2 * c)
                    A.copy(sa_sb_[h], ch_sa[h]).then_inc(sa_ok, 1)

            def chain_out(c, p, i, ctx_pair):
                act.wait_ge(ho_ok, 4 * c + 4)
                n = 2 * c
                dst = (io["state_out"][j] if ctx_pair else g.state)[bass.ds(n, 2)].rearrange("s p d n -> p s d n")
                act.dma_start(dst, hout[p].rearrange("p (s d) n -> p s d n", s=2)).then_inc(h_stored[p], 16)
                for h in range(2):
                    act.wait_ge(y_mm, 2 * c + h + 1)
                    if h == 0:
                        act.wait_ge(y_stored[p], 16 * i)
                    A.copy(ystage[p][rows[h]], b_ch[h][rows[h]]).then_inc(y_ok, 1)
                act.wait_ge(y_ok, 2 * c + 2)
                act.dma_start(g.scan_y[bass.ds(n, 2)].rearrange("s p d n -> p s d n"),
                              ystage[p].rearrange("p (s d) n -> p s d n", s=2)).then_inc(y_stored[p], 16)

            def exps(q):
                act.wait_ge(d0_ok, q + 1)
                act.wait_ge(w_ok, 2 * q)
                act.wait_ge(wp_ok, 2 * q)
                s_ = -DECAY_SCALE
                for d, out, src, sign in ((0, eB, d1, -s_), (1, eB, d0, s_), (0, eA, d0, s_), (1, eA, d1, -s_),
                                          (0, eR, d1, s_), (1, eR, d0, -s_)):
                    A.activation(sd(out)[:, :, d, :], sd(src)[:, :, d, :], ACT.Exp, scale=sign).then_inc(exp_ok, 1)

            def factors(q, p):
                s_ = -DECAY_SCALE
                for d, out, src, col in ((0, f_in[p], cum, HD - 1), (1, f_out[p], cum, HD - 1), (0, f_out[p], d1, P - 1), (1, f_in[p], d1, P - 1)):
                    A.activation(out.rearrange("p (s d) -> p s d", s=2)[:, :, d], sd(src)[:, :, d, col], ACT.Exp, scale=s_).then_inc(fac_ok, 1)

            def tok(q, p):
                for t, (bk, dst) in enumerate(((b_u[0], tokB[p]), (b_u[1], tokK[p]), (b_x[0], tokV[p]))):
                    act.wait_ge(tok_mm, 3 * q + t + 1)
                    A.copy(dst, bk).then_inc(tok_ok, 1)

            exps(0)
            factors(0, 0)

            def pair(q, p, i):
                chain = not known(q) or q >= 1
                c = q - 1
                if chain:
                    chain_rhs(c)
                    chain_sa(c)
                if not known(q) or q + 1 < PAIRS:
                    exps(q + 1)
                if chain:
                    chain_out(c, 1 - p, i - 1 if p == 0 else i, known(q) and c < CTX_PAIRS)
                if not known(q) or q + 1 < PAIRS:
                    factors(q + 1, 1 - p)
                tok(q, p)
            each_pair(act, pair)
            c = PAIRS - 1
            chain_rhs(c)
            chain_sa(c)
            chain_out(c, 1, PAIRS // 2 - 1, False)
            for p in range(2):
                act.wait_ge(y_stored[p], 16 * (PAIRS // 2))
                act.wait_ge(h_stored[p], 16 * (PAIRS // 2))

        @block.vector
        def _(dve):
            def prep_a(q, p, i):
                dve.wait_ge(raw_in[p], 112 * i + 112)
                dve.wait_ge(exp_ok, 6 * q)
                dve.wait_ge(fac_ok, 4 * q)
                flat = lambda a: a.rearrange("p a n -> p (a n)")
                V.tensor_tensor_scan(flat(cum), reset, raw[p][:, R_SW].rearrange("p a n -> p (a n)"), 0.0, op0=ALU.mult, op1=ALU.add).then_inc(scan_ok, 1)
                dve.wait_ge(scan_ok, q + 1)
                V.tensor_tensor(d1, cum, cum[:, :, HD - 1:HD].to_broadcast([P, 4, P]), op=ALU.subtract).then_inc(d1_ok, 1)
                dve.wait_ge(d1_ok, q + 1)
                V.tensor_tensor(d0, d1, raw[p][:, R_SW], op=ALU.subtract).then_inc(d0_ok, 1)
                dve.wait_ge(w_ok, 2 * q)
                dve.wait_ge(wp_ok, 2 * q)
                for u in range(4):
                    V.tensor_scalar(kd[:, u, :], raw[p][:, R_A, u, :], -1.0, ka[p][:, u:u + 1], ALU.add, ALU.mult).then_inc(t_ok, 1)
                dve.wait_ge(t_ok, 4 * q + 4)
                V.scalar_tensor_tensor(kd, kd, 1.0, raw[p][:, R_K], op0=ALU.add, op1=ALU.mult).then_inc(kd_ok, 1)
                V.tensor_tensor(bb, raw[p][:, R_KK], raw[p][:, R_A], op=ALU.mult).then_inc(b_ok, 1)

            def prep_b(q, p):
                dve.wait_ge(b_ok, q + 1)
                dve.wait_ge(exp_ok, 6 * q + 2)
                if not known(q) or q >= 2:
                    dve.wait_ge(y_mm, 2 * q - 2)
                V.tensor_tensor(wB[p], bb, eB, op=ALU.mult).then_inc(w_ok, 1)
                dve.wait_ge(exp_ok, 6 * q + 4)
                V.scalar_tensor_tensor(wA[p], raw[p][:, R_KK], -1.0, eA, op0=ALU.mult, op1=ALU.mult).then_inc(w_ok, 1)

            def start_state(c, p, i, ctx_pair):
                dve.wait_ge(y_mm, 2 * c)
                dve.wait_ge(fac_ok, 4 * c + 4)
                if not ctx_pair:
                    dve.wait_ge(hin_in[p], 16 * (i - CTX_PAIRS // 2) + 16)
                for u in range(4):
                    if ctx_pair:
                        V.memset(hs[:, u, :], 0.0).then_inc(hs_ok, 1)
                    else:
                        V.tensor_scalar(hs[:, u, :], hin[p][:, u, :], f_in[p][:, u:u + 1], None, ALU.mult).then_inc(hs_ok, 1)

            def new_state(c, p, i):
                dve.wait_ge(hs_ok, 4 * c + 4)
                dve.wait_ge(ho_ok, 4 * c)
                for h in range(2):
                    dve.wait_ge(st_mm, 2 * c + h + 1)
                    V.tensor_tensor(hn[rows[h]], ch_rhs[h][rows[h]], hs[rows[h]], op=ALU.add).then_inc(hn_ok, 1)
                dve.wait_ge(hn_ok, 2 * c + 2)
                dve.wait_ge(h_stored[p], 16 * i)
                for u in range(4):
                    V.tensor_scalar(hout[p][:, u, :], hn[:, u, :], f_out[p][:, u:u + 1], None, ALU.mult).then_inc(ho_ok, 1)

            def pair(q, p, i):
                chain = not known(q) or q >= 1
                c = q - 1
                ci = (i - 1 if p == 0 else i)
                nxt = not known(q) or q + 1 < PAIRS
                for h in range(2):
                    dve.wait_ge(gram_mm, 4 * q + h + 1)
                    V.tensor_tensor(sd(tab_t[h]), sd(b_u[h]), mask("strict"), op=ALU.mult).then_inc(tab_ok, 1)
                for h in range(2):
                    dve.wait_ge(tab_ok, 2 * q + h + 1)
                    V.tensor_tensor(sd(XT[h]), sd(tab_t[h]), mask("lv0t"), op=ALU.mult).then_inc(x0_ok, 1)
                    dve.wait_ge(gram_mm, 4 * q + 2 + h + 1)
                    V.tensor_tensor(sd(X[h]), sd(b_x[h]), mask("lv0"), op=ALU.mult).then_inc(x0_ok, 1)
                for h in range(2):
                    dve.wait_ge(x0_ok, 4 * q + 2 * h + 2)
                    V.tensor_tensor(sd(XT[h]), sd(XT[h]), mask("eye"), op=ALU.add).then_inc(eye_ok, 1)
                    V.tensor_tensor(sd(X[h]), sd(X[h]), mask("eye"), op=ALU.add).then_inc(eye_ok, 1)
                if chain:
                    start_state(c, 1 - p, ci, known(q) and c < CTX_PAIRS)
                for k in range(1, LEVELS):
                    for h in range(2):
                        dve.wait_ge(u_mm, 12 * q + 2 * (k - 1) + h + 1)
                        if k >= 2:
                            dve.wait_ge(x_mm, 12 * q + 2 * (k - 2) + h + 1)
                        V.tensor_tensor(sd(U[h]), sd(b_u[h]), mask(f"lv{k}"), op=ALU.mult).then_inc(u_ok, 1)
                    for h in range(2):
                        dve.wait_ge(x_mm, 12 * q + 2 * (k - 1) + h + 1)
                        if k < LEVELS - 1:
                            V.tensor_tensor(X[h], b_x[h], X[h], op=ALU.add).then_inc(xa_ok, 1)
                            V.tensor_tensor(XT[h], b_xt[h], XT[h], op=ALU.add).then_inc(xt_ok, 1)
                        else:
                            if not known(q) or q >= 2:
                                dve.wait_ge(sa_mm, 2 * q - 2)
                            V.tensor_tensor(inv_t[p][h], b_xt[h], XT[h], op=ALU.add).then_inc(xt_ok, 1)
                    if k == 1 and nxt:
                        prep_a(q + 1, 1 - p, i if p == 0 else i + 1)
                    if k == 3 and chain:
                        new_state(c, 1 - p, ci)
                    if k == 5 and nxt:
                        prep_b(q + 1, 1 - p)
                if not known(q) or q >= 2:
                    dve.wait_ge(y_mm, 2 * q - 2)
                for t, (bk, dst, m) in enumerate(((b_u, tak_t, "strict"), (b_x, trb_t, "incl"), (b_xt, trk_t, "incl"))):
                    for h in range(2):
                        dve.wait_ge(late_mm, 6 * q + 2 * t + h + 1)
                        V.tensor_tensor(sd(dst[p][h]), sd(bk[h]), mask(m), op=ALU.mult).then_inc(late_ok, 1)

            dve.wait_ge(const_in, 32)
            prep_a(0, 0, 0)
            prep_b(0, 0)
            each_pair(dve, pair)
            start_state(PAIRS - 1, 1, PAIRS // 2 - 1, False)
            new_state(PAIRS - 1, 1, PAIRS // 2 - 1)

        @block.gpsimd
        def _(pool):
            def prep(q, p):
                pool.wait_ge(kd_ok, q + 1)
                pool.wait_ge(exp_ok, 6 * q + 6)
                if not known(q) or q >= 2:
                    pool.wait_ge(y_mm, 2 * q - 2)
                nc.gpsimd.tensor_tensor(wK[p], kd, eB, op=ALU.mult).then_inc(wp_ok, 1)
                nc.gpsimd.tensor_tensor(wR[p], raw[p][:, R_R], eR, op=ALU.mult).then_inc(wp_ok, 1)

            prep(0, 0)

            def pair(q, p, i):
                if not known(q) or q + 1 < PAIRS:
                    prep(q + 1, 1 - p)
            each_pair(pool, pair)


def phase_rwkv_finish(nc, g, j):
    og = g.big[0]
    load = [g.big[1], g.big[2]]
    YF, YB, RR, KK_, VV, GG, A0, A1 = range(8)
    t = g.big[3]
    asum, p = [t[:, i, :] for i in range(2)], [t[:, 2 + i, :] for i in range(2)]
    yy, root = t[:, 4, :], t[:, 5, :]
    sq, yn = t[:, 6, :], t[:, 7, :]
    sig, bonus = g.stage[:, 0, :], g.stage[:, 1, :]
    V, A = nc.vector, nc.scalar
    with ExitStack() as ctx:
        sem = Sems(nc, ctx)
        y_ok, mean_mm, yc_ok, sq_ok, var_mm, root_ok, inv_ok, yn_ok, ya_ok, as_ok, t_ok, kd_ok, p_ok, bonus_mm, bonus_ok, y2_ok, sig_ok, silu_ok, out_ok = sem(
            "y_ok", "mean_mm", "yc_ok", "sq_ok", "var_mm", "root_ok", "inv_ok", "yn_ok", "ya_ok", "as_ok", "t_ok", "kd_ok", "p_ok", "bonus_mm",
            "bonus_ok", "y2_ok", "sig_ok", "silu_ok", "out_ok")
        in_ = [sem(f"block_in{i}") for i in range(2)]
        block = ctx.enter_context(nc.Block())

        @block.sync
        def _(sp):
            for b in range(NB):
                if b >= 2:
                    sp.wait_ge(out_ok, b - 1)
                dst = lambda i: load[b % 2][:, i, :].rearrange("p (t n) -> p t n", n=P)
                sp.dma_start(dst(YF), g.scan_y[b::NB, :, 0].rearrange("t p n -> p t n")).then_inc(in_[b % 2], 16)
                sp.dma_start(dst(YB)[:, 0], g.scan_y[NB - 1 - b, :, 1]).then_inc(in_[b % 2], 16)
                for i in range(1, NT):
                    sp.dma_start(dst(YB)[:, i], g.scan_y[NB * (NT - i) + NB - 1 - b, :, 1]).then_inc(in_[b % 2], 16)
                for i, a in ((RR, A_R), (KK_, A_K), (VV, A_V), (GG, A_G), (A0, A_A0), (A1, A_A1)):
                    sp.dma_start(dst(i), g.scan_in[b::NB, a].rearrange("t p n -> p t n")).then_inc(in_[b % 2], 16)

        @block.tensor
        def _(pe):
            def heads(src, banks, done):
                for c in range(CH):
                    mm = pe.matmul(g.ps[:, banks + c, 0:CW] if banks < 6 else g.ps[:, 6, 0:CW], g.head_ones[:, :],
                                   src[:, c * CW:(c + 1) * CW], start=True, stop=True)
                mm.then_inc(done, 1)
            for b in range(NB):
                pe.wait_ge(y_ok, b + 1)
                if b:
                    pe.wait_ge(root_ok, b)
                heads(yy, 0, mean_mm)
                pe.wait_ge(p_ok, b + 1)
                if b:
                    pe.wait_ge(bonus_ok, b)
                heads(p[b % 2], 3, bonus_mm)
                pe.wait_ge(sq_ok, b + 1)
                heads(sq, 0, var_mm)

        @block.scalar
        def _(act):
            for b in range(NB):
                act.wait_ge(in_[b % 2], 256 * (b // 2 + 1))
                if b:
                    act.wait_ge(silu_ok, b)
                    act.wait_ge(out_ok, b)
                A.activation(sig, load[b % 2][:, GG, :], ACT.Sigmoid).then_inc(sig_ok, 1)
                act.wait_ge(yc_ok, b + 1)
                if b:
                    act.wait_ge(var_mm, b)
                A.activation(sq, yy, ACT.Square).then_inc(sq_ok, 1)
                act.wait_ge(var_mm, b + 1)
                if b:
                    act.wait_ge(inv_ok, b)
                A.activation(as3(root), slot_view(g.ps[:, 0:3, :]), ACT.Sqrt, bias=g.eps[:, 0:1], scale=1.0 / HD).then_inc(root_ok, 1)

        @block.vector
        def _(dve):
            for b in range(NB):
                ld = load[b % 2]
                dve.wait_ge(in_[b % 2], 256 * (b // 2 + 1))
                if b:
                    dve.wait_ge(yn_ok, b)
                V.tensor_tensor(yy, ld[:, YF, :], ld[:, YB, :], op=ALU.add).then_inc(y_ok, 1)
                dve.wait_ge(as_ok, b + 1)
                V.tensor_scalar(asum[b % 2], asum[b % 2], -2.0, ch(g, "k_a", 8 * j + b), ALU.add, ALU.mult).then_inc(t_ok, 1)
                dve.wait_ge(t_ok, b + 1)
                V.scalar_tensor_tensor(asum[b % 2], asum[b % 2], 2.0, ld[:, KK_, :], op0=ALU.add, op1=ALU.mult).then_inc(kd_ok, 1)
                dve.wait_ge(kd_ok, b + 1)
                V.scalar_tensor_tensor(p[b % 2], asum[b % 2], ch(g, "r_k", 8 * j + b), ld[:, RR, :], op0=ALU.mult, op1=ALU.mult).then_inc(p_ok, 1)
                dve.wait_ge(mean_mm, b + 1)
                V.scalar_tensor_tensor(as3(yy), slot_view(g.ps[:, 0:3, :]), -1.0 / HD, as3(yy), op0=ALU.mult, op1=ALU.add).then_inc(yc_ok, 1)
                dve.wait_ge(bonus_mm, b + 1)
                if b:
                    dve.wait_ge(y2_ok, b)
                V.tensor_tensor(as3(bonus), slot_view(g.ps[:, 3:6, :]), as3(ld[:, VV, :]), op=ALU.mult).then_inc(bonus_ok, 1)
                dve.wait_ge(root_ok, b + 1)
                V.reciprocal(root, root).then_inc(inv_ok, 1)
                dve.wait_ge(inv_ok, b + 1)
                dve.wait_ge(yc_ok, b + 1)
                V.tensor_tensor(yn, yy, root, op=ALU.mult).then_inc(yn_ok, 1)
                dve.wait_ge(yn_ok, b + 1)
                V.tensor_scalar(yn, yn, ch(g, "gn_w", 8 * j + b), ch(g, "gn_b", 8 * j + b), ALU.mult, ALU.add).then_inc(ya_ok, 1)
                dve.wait_ge(ya_ok, b + 1)
                dve.wait_ge(bonus_ok, b + 1)
                V.tensor_tensor(yn, yn, bonus, op=ALU.add).then_inc(y2_ok, 1)
                dve.wait_ge(y2_ok, b + 1)
                dve.wait_ge(silu_ok, b + 1)
                V.tensor_tensor(og[:, b, :], yn, sig, op=ALU.mult).then_inc(out_ok, 1)
            dve.wait_ge(out_ok, NB)

        @block.gpsimd
        def _(pool):
            for b in range(NB):
                ld = load[b % 2]
                pool.wait_ge(in_[b % 2], 256 * (b // 2 + 1))
                if b >= 2:
                    pool.wait_ge(p_ok, b - 1)
                nc.gpsimd.tensor_tensor(asum[b % 2], ld[:, A0, :], ld[:, A1, :], op=ALU.add).then_inc(as_ok, 1)
                pool.wait_ge(sig_ok, b + 1)
                nc.gpsimd.tensor_tensor(sig, sig, ld[:, GG, :], op=ALU.mult).then_inc(silu_ok, 1)


def attn_memory(g):
    rest = g.big[3].rearrange("p b t -> p (b t)")
    keys = rest[:, 0:2560].rearrange("p (b t) -> p b t", b=2)
    vals = rest[:, 2560:5120].rearrange("p (t n) -> p t n", n=256)
    wv = rest[:, 5120:7168].rearrange("p (k n) -> p k n", n=256)
    cos = rest[:, 7168:8192]
    sin = rest[:, 8192:9216]
    return keys, vals, wv, cos, sin


def phase_attention_project(nc, g):
    h, q, sg = g.big[0], g.big[1], g.big[2]
    keys, vals, wv, cos, sin = attn_memory(g)
    sq, inv, t1 = g.stage[:, 0, :], g.stage[:, 1, :], g.extra[:, 0:T]
    rot = g.extra[:, T:T + P]
    base = w_base("attn")
    V, A = nc.vector, nc.scalar
    QK = NB + 2
    with ExitStack() as ctx:
        sem = Sems(nc, ctx)
        v_in, tab_in, ctx_in, v_mm, v_ok, out_st, proj_done, sq_ok, norm_mm, rot_mm, ms_ok, root_ok, inv_ok, c_ok, s_ok, t_ok, q_ok, sig_ok, silu_ok, qw_ok = sem(
            "v_in", "tab_in", "ctx_in", "v_mm", "v_ok", "out_st", "proj_done", "sq_ok", "norm_mm", "rot_mm", "ms_ok", "root_ok",
            "inv_ok", "c_ok", "s_ok", "t_ok", "q_ok", "sig_ok", "silu_ok", "qw_ok")
        slab_in = [sem(f"slab_in{i}") for i in range(WSLOTS)]
        block = ctx.enter_context(nc.Block())
        dest = lambda n: q[:, n, :] if n < NB else keys[:, n - NB, 0:T]
        LC = LAT // 2

        @block.sync
        def _(sp):
            sp.dma_start(wv, g.io["wv"]).then_inc(v_in, 16)
            sp.dma_start(cos, g.io["cos"]).then_inc(tab_in, 16)
            sp.dma_start(sin, g.io["sin"]).then_inc(tab_in, 16)
            sp.dma_start(rot, g.io["rot"]).then_inc(tab_in, 16)
            sp.dma_start(keys[:, :, T:T + P], g.io["ck"]).then_inc(ctx_in, 16)
            sp.dma_start(vals[:, NT, :], g.io["cv"]).then_inc(ctx_in, 16)
            load_slabs(sp, g, base, 18, slab_in, proj_done)
            sp.wait_ge(q_ok, 2 * QK)
            sp.dma_start(g.io["k_out"], keys[:, :, 0:P]).then_inc(out_st, 16)
            sp.wait_ge(v_ok, 1)
            sp.dma_start(g.io["v_out"], vals[:, 0, :]).then_inc(out_st, 16)
            sp.wait_ge(out_st, 32)
            sp.wait_ge(ctx_in, 32)

        @block.tensor
        def _(pe):
            pe.wait_ge(v_in, 16)
            for t in range(NT):
                if t >= 2:
                    pe.wait_ge(v_ok, t - 1)
                for k in range(NB):
                    mm = pe.matmul(g.ps[:, 6 + t % 2, 0:256], h[:, k, t * P:(t + 1) * P], wv[:, k, :], start=k == 0, stop=k == NB - 1)
                mm.then_inc(v_mm, 1)

            def proj(n):
                pe.wait_ge(slab_in[n % WSLOTS], 16 * (n // WSLOTS + 1))
                if 1 <= n <= QK:
                    pe.wait_ge(qw_ok, n)
                    pe.wait_ge(sq_ok, n)
                elif n:
                    pe.wait_ge(silu_ok, n - QK)
                multiply(pe, g, h, n % WSLOTS, 0, proj_done)

            def norm_rot(n):
                pe.wait_ge(sq_ok, n + 1)
                if n:
                    pe.wait_ge(ms_ok, n)
                    pe.wait_ge(s_ok, n)
                for c in range(CH):
                    mm = pe.matmul(g.ps[:, 3 + c, 0:CW], g.head_ones[:, :], sq[:, c * CW:(c + 1) * CW], start=True, stop=True)
                mm.then_inc(norm_mm, 1)
                pe.wait_ge(qw_ok, n + 1)
                for c in range(2):
                    mm = pe.matmul(g.ps[:, 6 + c, :], rot, dest(n)[:, CTX + c * LC:CTX + (c + 1) * LC], start=True, stop=True)
                mm.then_inc(rot_mm, 1)

            pe.wait_ge(v_ok, NT)
            pe.wait_ge(tab_in, 48)
            for n in range(QK):
                proj(n)
                if n:
                    norm_rot(n - 1)
            proj(QK)
            norm_rot(QK - 1)
            for n in range(QK + 1, 18):
                proj(n)

        @block.scalar
        def _(act):
            for t in range(NT):
                act.wait_ge(v_mm, t + 1)
                A.copy(vals[:, t, :], g.ps[:, 6 + t % 2, 0:256]).then_inc(v_ok, 1)
            for n in range(QK):
                act.wait_ge(proj_done, n + 1)
                w = ch(g, "q_norm" if n < NB else "k_norm", 0)
                A.activation(as3(dest(n)), slot_view(g.ps[:, 0:3, :]), ACT.Copy, scale=w).then_inc(qw_ok, 1)
                if n:
                    act.wait_ge(norm_mm, n)
                A.activation(as3(sq), slot_view(g.ps[:, 0:3, :]), ACT.Square).then_inc(sq_ok, 1)
                if n:
                    act.wait_ge(ms_ok, n)
                    A.activation(inv, inv, ACT.Sqrt).then_inc(root_ok, 1)
            act.wait_ge(ms_ok, QK)
            A.activation(inv, inv, ACT.Sqrt).then_inc(root_ok, 1)
            for n in range(NB):
                act.wait_ge(proj_done, QK + n + 1)
                if n:
                    act.wait_ge(silu_ok, n)
                else:
                    act.wait_ge(norm_mm, QK)
                A.activation(as3(sq), slot_view(g.ps[:, 0:3, :]), ACT.Sigmoid).then_inc(sig_ok, 1)

        @block.vector
        def _(dve):
            for n in range(QK):
                dve.wait_ge(norm_mm, n + 1)
                V.tensor_scalar(as3(inv), slot_view(g.ps[:, 3:6, :]), 1.0 / HD, RMS_EPS, ALU.mult, ALU.add).then_inc(ms_ok, 1)
                dve.wait_ge(root_ok, n + 1)
                V.reciprocal(inv, inv).then_inc(inv_ok, 1)
                dve.wait_ge(rot_mm, n + 1)
                lat = dest(n)[:, CTX:T]
                V.tensor_tensor(t1[:, 0:LAT].rearrange("p (c n) -> p c n", c=2), g.ps[:, 6:8, :],
                                sin.rearrange("p (c n) -> p c n", c=2), op=ALU.mult).then_inc(s_ok, 1)
                V.tensor_tensor(lat, lat, cos, op=ALU.mult).then_inc(c_ok, 1)
                dve.wait_ge(s_ok, n + 1)
                dve.wait_ge(c_ok, n + 1)
                V.tensor_tensor(t1[:, 0:LAT], t1[:, 0:LAT], lat, op=ALU.add).then_inc(t_ok, 1)
                dve.wait_ge(t_ok, n + 1)
                dve.wait_ge(inv_ok, n + 1)
                V.tensor_tensor(lat, t1[:, 0:LAT], inv[:, CTX:T], op=ALU.mult).then_inc(q_ok, 1)
                V.tensor_tensor(dest(n)[:, 0:CTX], dest(n)[:, 0:CTX], inv[:, 0:CTX], op=ALU.mult).then_inc(q_ok, 1)
                dve.wait_ge(q_ok, 2 * n + 2)
            for n in range(NB):
                dve.wait_ge(sig_ok, n + 1)
                V.tensor_tensor(as3(sg[:, n, :]), slot_view(g.ps[:, 0:3, :]), as3(sq), op=ALU.mult).then_inc(silu_ok, 1)
                dve.wait_ge(silu_ok, n + 1)


def phase_attention(nc, g):
    q, sg = g.big[1], g.big[2]
    keys, vals, _, _, _ = attn_memory(g)
    free = g.big[0].rearrange("p b t -> p (b t)")
    qz = [[free[:, (2 * i + h) * T:(2 * i + h + 1) * T] for h in range(2)] for i in range(2)]
    prob = [free[:, (4 + i) * T:(5 + i) * T] for i in range(2)]
    prob_t = [free[:, (6 + i) * T:(7 + i) * T] for i in range(2)]
    small = g.extra
    nmax, bias, rsum, rinv = [[small[:, 4 * k + i:4 * k + i + 1] for i in range(2)] for k in range(4)]
    V, A = nc.vector, nc.scalar
    SCALE = HD ** -0.5
    UNITS = 2 * NT
    rows = [slice(0, HD), slice(HD, P)]
    with ExitStack() as ctx:
        sem = Sems(nc, ctx)
        zero_ok, qz_ok, sc_mm, max_ok, bias_ok, exp_ok, rinv_ok, p_ok, tr_mm, tr_ok, pv_mm, o_ok = sem(
            "zero_ok", "qz_ok", "sc_mm", "max_ok", "bias_ok", "exp_ok", "rinv_ok", "p_ok", "tr_mm", "tr_ok", "pv_mm", "o_ok")
        block = ctx.enter_context(nc.Block())

        def batches(t):
            return ((0, 1),) if t == 0 else ((0, 4), (4, 4), (8, 1))

        BATCHES = 2 * (1 + 3 * NLT)

        def batch_at(u):
            return sum(len(batches(v // 2)) for v in range(u))

        @block.gpsimd
        def _(pool):
            for i in range(2):
                for h in range(2):
                    nc.gpsimd.memset(qz[i][h], 0.0).then_inc(zero_ok, 1)
            pool.wait_ge(zero_ok, 4)
            for b in range(NB):
                i = b % 2
                if b >= 2:
                    pool.wait_ge(sc_mm, UNITS * (b - 1))
                for h in range(2):
                    nc.gpsimd.tensor_copy(qz[i][h][rows[h]], q[rows[h], b, :]).then_inc(qz_ok, 1)

        @block.tensor
        def _(pe):
            def scores(b, i, kv, u):
                t, h = u // 2, u % 2
                s = u % 2
                n = UNITS * b + u
                if u == 0:
                    pe.wait_ge(qz_ok, 2 * b + 2)
                if not isinstance(b, int) or n >= 2:
                    pe.wait_ge(o_ok, n - 1)
                lhs = qz[i][h][:, t * P:(t + 1) * P]
                if t == 0:
                    mm = pe.matmul(g.ps[:, 3 * s, 0:P], lhs, keys[:, kv, 0:P], start=True, stop=True)
                else:
                    for c in range(CH):
                        mm = pe.matmul(g.ps[:, 3 * s + c, 0:CW], lhs, keys[:, kv, CTX + c * CW:CTX + (c + 1) * CW], start=True, stop=True)
                mm.then_inc(sc_mm, 1)

            def values(b, kv, u):
                t, h = u // 2, u % 2
                s = u % 2
                n = UNITS * b + u
                bt = BATCHES * b + batch_at(u)
                pe.wait_ge(p_ok, n + 1)
                for m, (k0, kn) in enumerate(batches(t)):
                    bk = 6 + (batch_at(u) + m) % 2
                    if not isinstance(b, int) or b > 0 or batch_at(u) + m >= 2:
                        pe.wait_ge(tr_ok, bt + m - 1)
                    for k in range(kn):
                        mm = pe.transpose(g.ps[:, bk, k * P:(k + 1) * P], prob[s][:, (k0 + k) * P:(k0 + k + 1) * P], g.ident[:, :])
                    mm.then_inc(tr_mm, 1)
                nk = 1 if t == 0 else 9
                for m, (k0, kn) in enumerate(batches(t)):
                    pe.wait_ge(tr_ok, bt + m + 1)
                    for k in range(k0, k0 + kn):
                        tile = 0 if t == 0 else 1 + k
                        mm = pe.matmul(g.ps[rows[h], 3 * s, CW:512], vals[:, tile, (2 * kv + h) * HD:(2 * kv + h + 1) * HD],
                                       prob_t[s][:, k * P:(k + 1) * P], start=k == 0, stop=k == nk - 1)
                mm.then_inc(pv_mm, 1)

            def blocks(b, i, kv):
                scores(b, i, kv, 0)
                for u in range(UNITS):
                    if u + 1 < UNITS:
                        scores(b, i, kv, u + 1)
                    values(b, kv, u)

            blocks(0, 0, 0)
            blocks(1, 1, 0)
            blocks(2, 0, 0)
            blocks(3, 1, 0)
            with pe.Fori(2, 4) as r:
                for i in range(2):
                    blocks(2 * r + i, i, 1)

        def soft_loops(eng, fn):
            with eng.Fori(1, 4) as r:
                for i in range(2):
                    fn(2 * r + i, i)

        @block.scalar
        def _(act):
            def head(b, u):
                t, s = u // 2, u % 2
                n = UNITS * b + u
                act.wait_ge(bias_ok, n + 1)
                if not isinstance(b, int) or n >= 2:
                    act.wait_ge(pv_mm, n - 1)
                src = g.ps[:, 3 * s, 0:P] if t == 0 else slot_view(g.ps[:, 3 * s:3 * s + 3, :])
                dst = prob[s][:, 0:P] if t == 0 else as3(prob[s])
                A.activation(dst, src, ACT.Exp, bias=bias[s], scale=SCALE, accum_out=rsum[s]).then_inc(exp_ok, 1)

            def tail(b, u):
                t, s = u // 2, u % 2
                bt = BATCHES * b + batch_at(u)
                for m, (k0, kn) in enumerate(batches(t)):
                    act.wait_ge(tr_mm, bt + m + 1)
                    bk = 6 + (batch_at(u) + m) % 2
                    A.copy(prob_t[s][:, k0 * P:(k0 + kn) * P], g.ps[:, bk, 0:kn * P]).then_inc(tr_ok, 1)

            def blocks(b, i):
                head(b, 0)
                for u in range(UNITS):
                    if u + 1 < UNITS:
                        head(b, u + 1)
                    tail(b, u)
            blocks(0, 0)
            blocks(1, 1)
            soft_loops(act, blocks)

        @block.vector
        def _(dve):
            def head(b, u):
                t, s = u // 2, u % 2
                n = UNITS * b + u
                dve.wait_ge(sc_mm, n + 1)
                if t == 0:
                    V.tensor_reduce(nmax[s], g.ps[:, 3 * s, 0:P], mybir.AxisListType.X, ALU.max).then_inc(max_ok, 1)
                else:
                    V.tensor_reduce(nmax[s], slot_view(g.ps[:, 3 * s:3 * s + 3, :]), mybir.AxisListType.XY, ALU.max).then_inc(max_ok, 1)
                dve.wait_ge(max_ok, n + 1)
                if not isinstance(b, int) or n >= 2:
                    dve.wait_ge(exp_ok, n - 1)
                V.tensor_scalar(bias[s], nmax[s], -SCALE, None, ALU.mult).then_inc(bias_ok, 1)

            def mid(b, u):
                t, s = u // 2, u % 2
                n = UNITS * b + u
                w = P if t == 0 else T
                dve.wait_ge(exp_ok, n + 1)
                V.reciprocal(rinv[s], rsum[s]).then_inc(rinv_ok, 1)
                dve.wait_ge(rinv_ok, n + 1)
                V.tensor_scalar(prob[s][:, 0:w], prob[s][:, 0:w], rinv[s], None, ALU.mult).then_inc(p_ok, 1)

            def tail(b, u):
                t, h = u // 2, u % 2
                n = UNITS * b + u
                dve.wait_ge(pv_mm, n + 1)
                gate = (sg[rows[h], b, t * P:(t + 1) * P] if isinstance(b, int)
                        else sg[rows[h], bass.ds(b, 1), t * P:(t + 1) * P].rearrange("p o n -> p (o n)"))
                V.tensor_tensor(gate, g.ps[rows[h], 3 * (u % 2), CW:512], gate, op=ALU.mult).then_inc(o_ok, 1)

            def blocks(b, i):
                head(b, 0)
                for u in range(UNITS):
                    if u + 1 < UNITS:
                        head_wait = u + 1
                        if u >= 1:
                            tail(b, u - 1)
                        mid(b, u)
                        head(b, head_wait)
                    else:
                        tail(b, u - 1)
                        mid(b, u)
                        tail(b, u)
            blocks(0, 0)
            blocks(1, 1)
            soft_loops(dve, blocks)
            dve.wait_ge(o_ok, NB * UNITS)


def phase_conv(nc, g):
    h, og = g.big[0], g.big[1]
    t = g.big[2]
    cs, uu, cv, gg, sig = [t[:, i, :] for i in range(5)]
    V, A = nc.vector, nc.scalar
    with ExitStack() as ctx:
        sem = Sems(nc, ctx)
        proj_done, evacuated, c_ok, u_ok, w1_ok, w0_ok, w2_ok, b_ok, sig_ok, silu_ok, out_ok = sem(
            "proj_done", "evacuated", "c_ok", "u_ok", "w1_ok", "w0_ok", "w2_ok", "b_ok", "sig_ok", "silu_ok", "out_ok")
        slab_in = [sem(f"slab_in{i}") for i in range(WSLOTS)]
        block = ctx.enter_context(nc.Block())

        @block.sync
        def _(sp):
            load_slabs(sp, g, w_base("conv"), 4 * NB, slab_in, proj_done)

        @block.tensor
        def _(pe):
            def block_of(b, first=False):
                for u in range(4):
                    pe.wait_ge(slab_in[u % 2], 32 * b + 16 * (u // 2) + 16)
                    if u == 2:
                        pe.wait_ge(c_ok, b + 1)
                    elif u == 3:
                        pe.wait_ge(evacuated, 3 * b + 1)
                    elif not first:
                        pe.wait_ge(evacuated, 3 * b - 1 + u)
                    multiply(pe, g, h, u % 2, 3 * (u % 2), proj_done)
            block_of(0, True)
            with pe.Fori(1, NB) as b:
                block_of(b)

        @block.scalar
        def _(act):
            for b in range(NB):
                act.wait_ge(proj_done, 4 * b + 1)
                if b:
                    act.wait_ge(u_ok, b)
                A.copy(as3(cs), slot_view(g.ps[:, 0:3, :])).then_inc(c_ok, 1)
                act.wait_ge(proj_done, 4 * b + 4)
                if b:
                    act.wait_ge(silu_ok, b)
                A.activation(as3(sig), slot_view(g.ps[:, 3:6, :]), ACT.Sigmoid).then_inc(sig_ok, 1)

        @block.vector
        def _(dve):
            for b in range(NB):
                w = lambda i: ch(g, "conv_w", 8 * i + b)
                dve.wait_ge(proj_done, 4 * b + 2)
                dve.wait_ge(c_ok, b + 1)
                V.tensor_tensor(as3(uu), slot_view(g.ps[:, 3:6, :]), as3(cs), op=ALU.mult).then_inc(evacuated, 1)
                dve.wait_ge(evacuated, 3 * b + 1)
                V.tensor_scalar(cv, uu, w(1), ch(g, "conv_b", b), ALU.mult, ALU.add).then_inc(w1_ok, 1)
                dve.wait_ge(w1_ok, b + 1)
                for _, a0, a1 in token_ranges():
                    V.scalar_tensor_tensor(cv[:, a0 + 1:a1], uu[:, a0:a1 - 1], w(0), cv[:, a0 + 1:a1], op0=ALU.mult, op1=ALU.add).then_inc(w0_ok, 1)
                dve.wait_ge(w0_ok, 2 * b + 2)
                for i, (_, a0, a1) in enumerate(token_ranges()):
                    V.scalar_tensor_tensor(cv[:, a0:a1 - 1], uu[:, a0 + 1:a1], w(2), cv[:, a0:a1 - 1], op0=ALU.mult, op1=ALU.add).then_inc(w2_ok, 1)
                dve.wait_ge(w2_ok, 2 * b + 2)
                V.tensor_copy(g.flag[:, 2:3], g.flag[:, 1:2]).then_inc(u_ok, 1)
                dve.wait_ge(proj_done, 4 * b + 3)
                V.tensor_tensor(as3(cv), slot_view(g.ps[:, 0:3, :]), as3(cv), op=ALU.mult).then_inc(evacuated, 1)
                dve.wait_ge(evacuated, 3 * b + 2)
                dve.wait_ge(sig_ok, b + 1)
                V.tensor_tensor(as3(gg), slot_view(g.ps[:, 3:6, :]), as3(sig), op=ALU.mult).then_inc(evacuated, 1)
                dve.wait_ge(evacuated, 3 * b + 3)
                dve.wait_ge(u_ok, b + 1)
                V.tensor_tensor(og[:, b, :], cv, gg, op=ALU.mult).then_inc(silu_ok, 1)
                dve.wait_ge(silu_ok, b + 1)


def residual(nc, g, ada, tmp, b, x_ok):
    for c, a0, a1 in token_ranges():
        nc.vector.scalar_tensor_tensor(g.x[:, b, a0:a1], tmp[:, b, a0:a1], ada[:, 16 + b, c:c + 1], g.x[:, b, a0:a1],
                                       op0=ALU.mult, op1=ALU.add).then_inc(x_ok, 1)


def phase_output(nc, g, layer):
    kind = MIXER[layer]
    og = (g.big[0], g.big[2], g.big[1])[kind]
    base = (w_base("rwkv", layer // 3) + W_RWKV, w_base("attn") + 18, w_base("conv") + 32)[kind]
    m = g.big[3]
    tmp = g.big[0] if kind else g.big[1]
    work = (g.big[2], g.big[1], g.big[2])[kind]
    sq = [work[:, i, :] for i in range(2)]
    ms, root, rstd = work[:, 2, :], work[:, 3, :], work[:, 4, :]
    ada = g.ada[:, layer]
    V, A = nc.vector, nc.scalar
    with ExitStack() as ctx:
        sem = Sems(nc, ctx)
        proj_done, evacuated, sq_ok, sq_used, ms_ok, root_ok, rstd_ok, tmp_ok, x_ok = sem(
            "proj_done", "evacuated", "sq_ok", "sq_used", "ms_ok", "root_ok", "rstd_ok", "tmp_ok", "x_ok")
        slab_in = [sem(f"slab_in{i}") for i in range(WSLOTS)]
        block = ctx.enter_context(nc.Block())

        @block.sync
        def _(sp):
            load_slabs(sp, g, base, NB, slab_in, proj_done)

        @block.tensor
        def _(pe):
            project(pe, g, og, NB, 0, slab_in, evacuated, proj_done)
            pe.wait_ge(evacuated, NB)
            norm_matmuls(pe, g, sq, sq_ok, sq_used, 0)

        @block.scalar
        def _(act):
            for b in range(NB):
                act.wait_ge(proj_done, b + 1)
                A.copy(as3(m[:, b, :]), slot_view(g.ps[:, 3 * (b % 2):3 * (b % 2) + 3, :])).then_inc(evacuated, 1)
            act.wait_ge(evacuated, NB)
            for b in range(NB):
                if b >= 2:
                    act.wait_ge(sq_used, b - 1)
                A.activation(sq[b % 2], m[:, b, :], ACT.Square).then_inc(sq_ok, 1)
            act.wait_ge(ms_ok, 1)
            A.activation(root, ms, ACT.Sqrt).then_inc(root_ok, 1)

        @block.vector
        def _(dve):
            dve.wait_ge(sq_used, NB)
            V.tensor_scalar(as3(ms), slot_view(g.ps[:, 0:3, :]), 1.0 / D, RMS_EPS, ALU.mult, ALU.add).then_inc(ms_ok, 1)
            dve.wait_ge(root_ok, 1)
            V.reciprocal(rstd, root).then_inc(rstd_ok, 1)
            dve.wait_ge(rstd_ok, 1)
            for b in range(NB):
                V.tensor_tensor(tmp[:, b, :], m[:, b, :], rstd, op=ALU.mult).then_inc(tmp_ok, 1)
                if b:
                    dve.wait_ge(tmp_ok, b)
                    residual(nc, g, ada, tmp, b - 1, x_ok)
            dve.wait_ge(tmp_ok, NB)
            residual(nc, g, ada, tmp, NB - 1, x_ok)
            dve.wait_ge(x_ok, 2 * NB)



def phase_end(nc, g):
    with ExitStack() as ctx:
        stored = Sems(nc, ctx)("stored_y")
        block = ctx.enter_context(nc.Block())

        @block.sync
        def _(sp):
            sp.dma_start(g.io["y"], g.x[:, :, :]).then_inc(stored, 16)
            sp.wait_ge(stored, 16)


def constants():
    t = np.arange(P)
    row, col = t[:, None], t[None, :]
    out = {}
    masks = np.zeros((P, len(MASKS), 2, P), np.float32)

    def put(name, fwd, bwd):
        masks[:, MASKS[name], 0] = fwd
        masks[:, MASKS[name], 1] = bwd
    put("strict", row < col, row > col)
    put("incl", row <= col, row >= col)
    for k in range(LEVELS):
        n = 1 << k
        low = (row // n == col // n + 1) & ((row // n) % 2 == 1)
        put(f"lv{k}", low, low.T)
        if k == 0:
            put("lv0t", low.T, low)
    put("eye", row == col, row == col)
    out["masks"] = masks
    reset = np.ones((P, 4, P), np.float32)
    reset[:, :, 0] = 0
    out["reset"] = reset.reshape(P, 4 * P)
    out["ident"] = np.eye(P, dtype=np.float32)
    out["ones"] = np.ones((P, P), np.float32)
    out["head_ones"] = (row // HD == col // HD).astype(np.float32)
    f = HD // 4
    inv = np.float32(10000.0) ** (-np.arange(f, dtype=np.float32) / np.float32(f))
    pos = np.arange(LAT)
    axis = np.stack([pos // 64, pos % 64]).astype(np.float32)
    d = np.arange(P) % HD
    ang = axis[d // 32] * inv[d % f][:, None]
    out["cos"] = np.cos(ang).astype(np.float32)
    out["sin"] = np.sin(ang).astype(np.float32)
    rot = np.zeros((P, P), np.float32)
    for c in range(P):
        if (c % 32) < f:
            rot[c + f, c] = -1
        else:
            rot[c - f, c] = 1
    out["rot"] = rot
    return out


def columns(v):
    return np.asarray(v).reshape(-1, P).T


def slabs(w):
    e = w.shape[1]
    return w.reshape(NB, P, e // P, P).transpose(2, 1, 0, 3).reshape(e // P, P, NB * P)


def layout(i):
    f = {k: np.asarray(v) for k, v in i.items()}
    io = constants()
    x = np.concatenate([f["x_prompt"][0], f["x_sample"][0]])
    io["x"] = x.T.reshape(NB, P, T).transpose(1, 0, 2)
    io["cond"] = np.stack([f["c_ctx"], f["c"][0]], -1).reshape(NB, P, 2).transpose(1, 0, 2)
    io["w_ada"] = f["w_ada"].reshape(4, NB, P, 6, 512).transpose(0, 3, 2, 1, 4).reshape(24, P, NB, 512)
    hd = np.tile(f["attn_q_norm"][0], 2)[:, None], np.tile(f["attn_k_norm"][0], 2)[:, None]
    parts = dict(norm_pre=columns(f["norm_pre"]), norm_post=columns(f["norm_post"]), b_ada=columns(f["b_ada"]), mu=columns(f["rwkv_mu"]),
                 decay0=columns(f["rwkv_decay0"]), icl0=columns(f["rwkv_icl0"]), k_k=columns(f["rwkv_k_k"]), r_k=columns(f["rwkv_r_k"]),
                 gn_w=columns(f["rwkv_gn_w"]), gn_b=columns(f["rwkv_gn_b"]), k_a=columns(f["rwkv_k_a"]), q_norm=hd[0], k_norm=hd[1],
                 conv_w=columns(f["conv_w"]), conv_b=columns(f["conv_b"]))
    lay = chan_layout()
    io["chan"] = np.concatenate([parts[n] for n in lay if n != "_"], 1)
    order = [h for b in range(4) for h in (b, 4 + b)] + [h for b in range(4) for h in (8 + b, 12 + b)]
    cols = np.concatenate([np.arange(h * HD, (h + 1) * HD) for h in order])
    wi = f["attn_w_in"][0]
    w = []
    for j in range(2):
        w += [slabs(f["rwkv_w_in"][j, m]) for m in range(4)]
        w += [slabs(f[n][j].transpose(1, 0, 2).reshape(D, P)) for n in ("rwkv_decay1", "rwkv_icl1")]
        w.append(slabs(f["rwkv_w_out"][j]))
    w += [slabs(wi[:, cols]), slabs(wi[:, D:D + 256]), slabs(wi[:, D + 512:][:, cols]), slabs(f["attn_w_out"][0][cols])]
    cw = np.stack([slabs(f["conv_w_in"][0][:, a * D:(a + 1) * D]) for a in (1, 2, 0, 3)], 1)
    w += [cw.reshape(4 * NB, P, NB * P), slabs(f["conv_w_out"][0])]
    io["w"] = np.concatenate(w)
    up = np.zeros((2, P, 2, 2, NB, P), np.float32)
    for a, n in enumerate(("rwkv_decay2", "rwkv_icl2")):
        for z in range(2):
            up[:, z * 64:(z + 1) * 64, a, z] = f[n][:, z].reshape(2, 64, NB, P)
    io["lora_up"] = up.reshape(2, P, 32, P)
    io["wv"] = wi[:, D + 256:D + 512].reshape(NB, P, 256).transpose(1, 0, 2)
    io["ck"] = f["cache_k"][0, 0].reshape(P, 2, P).transpose(2, 1, 0)
    io["cv"] = f["cache_v"][0, 0].reshape(P, 256)
    st = f["state_rwkv"][0].transpose(0, 1, 2, 4, 3).reshape(2, 2, NB, P, HD)
    io["state_in"] = np.stack([st[:, 0], st[:, 1, ::-1]], 3)
    ka = f["rwkv_k_a"].reshape(2, NB, P)
    both = np.stack([ka, ka[:, ::-1]], -1)
    both = np.tile(both.reshape(2, 4, 2, P, 2), (1, NT, 1, 1, 1))
    io["ka"] = both.transpose(0, 1, 3, 2, 4).reshape(2, PAIRS, P, 4)
    return {k: np.ascontiguousarray(v) for k, v in io.items()}


OUTS = {"y": (P, NB, T), "state_out": (2, NB, P, 2, HD), "k_out": (P, 2, P), "v_out": (P, 256)}


def program(nc, arrays, **kw):
    io = {k: nc.dram_tensor(f"in_{k}", a.shape, F32, kind="ExternalInput").ap() for k, a in arrays.items()}
    io.update({k: nc.dram_tensor(f"out_{k}", s, F32, kind="ExternalOutput").ap() for k, s in OUTS.items()})
    build(nc, io, **kw)


def unpack(r):
    y = r["out_y"].transpose(1, 0, 2).reshape(D, T).T
    st = r["out_state_out"]
    fwd, bwd = st[:, :, :, 0], st[:, ::-1, :, 1]
    both = np.stack([fwd, bwd], 1).reshape(2, 2, 16, HD, HD).transpose(0, 1, 2, 4, 3)
    k = r["out_k_out"].transpose(2, 1, 0).reshape(1, 1, CTX, 4, HD)
    v = r["out_v_out"].reshape(1, 1, CTX, 4, HD)
    c = np.ascontiguousarray
    return c(y[None, :CTX]), c(y[None, CTX:]), c(both[None]), c(k), c(v)


def kernel(**inputs):
    import concourse.bacc as bacc
    from concourse.bass_utils import run_bass_kernel_spmd as run
    nc = bacc.Bacc("TRN2", target_bir_lowering=False, num_devices=1)
    arrays = layout(inputs)
    program(nc, arrays)
    r = run(nc, [{f"in_{k}": a for k, a in arrays.items()}], core_ids=[0])
    return unpack(r.results[0])
```

```python
from contextlib import ExitStack
import math

import numpy as np

import concourse.bass as bass
from concourse import mybir
from concourse.alu_op_type import AluOpType as ALU

ACT = mybir.ActivationFunctionType
F32 = mybir.dt.float32
F32R = mybir.dt.float32r

P = 128
D = 1024
NB = D // P
CTX = 128
LAT = 1024
T = CTX + LAT
NT = T // P
NLT = LAT // P
CH = 3
CW = T // CH
HD = 64
RMS_EPS = 1e-6
GN_EPS = 64e-5
DECAY_SCALE = math.exp(-0.5)
LEVELS = 7
WSLOTS = 2

MIXER = (0, 1, 2, 0)

A_SW0, A_A0, A_R, A_K, A_KK, A_V, A_SW1, A_A1, A_G = range(9)
R_SW, R_A, R_R, R_K, R_KK, R_V = range(6)


class Core:
    pass


def build(nc, io, layers=(0, 1, 2, 3)):
    g = Core()
    g.io = io
    dram = lambda name, shape: nc.dram_tensor(name, shape, F32, kind="Internal").ap()
    g.scan_in = dram("scan_in", (NT * NB, 9, P, P))
    g.scan_y = dram("scan_y", (NT * NB, P, 2, P))
    g.state = dram("state_chain", ((NT + 1) * NB, P, 2, HD))

    ctx = ExitStack()
    with ctx:
        sb = lambda name, shape: ctx.enter_context(nc.sbuf_tensor(name, shape, F32))
        g.x = sb("x_resid", [P, NB, T])

        def sb_both(name, shape):
            at = -(-nc.sbuf_base // 32) * 32
            plain = sb(name, shape)
            return plain, nc.alloc_sbuf_tensor_at(name + "_r", shape, F32R, offset=at)

        g.slab, g.slab_r = sb_both("w_slab", [P, WSLOTS, NB * P])
        arena_at = -(-nc.sbuf_base // 32) * 32
        g.arena = sb("arena", [P, 4 * NB * T])
        g.big_r = [nc.alloc_sbuf_tensor_at(f"big_r{i}", [P, NB, T], F32R, offset=arena_at + 4 * i * NB * T) for i in range(4)]
        g.stage, g.stage_r = sb_both("stage", [P, 2, T])
        g.ones = sb("ones", [P, P])
        g.ident = sb("ident", [P, P])
        g.extra = sb("extra", [P, T + P])
        g.eps = sb("eps", [P, 1])
        g.flag = sb("flag", [P, 4])
        g.head_ones = sb("head_ones", [P, P])
        g.ada = sb("ada", [P, 4, 24, 2])
        g.chan = sb("chan", [P, io["chan"].shape[1]])
        g.ps = ctx.enter_context(nc.psum_tensor("ps", [P, 8, 512], F32))
        n = NB * T
        g.big = [g.arena[:, i * n:(i + 1) * n].rearrange("p (b t) -> p b t", b=NB) for i in range(4)]

        phase_start(nc, g)
        for layer in layers:
            j = layer // 3
            phase_prenorm(nc, g, layer)
            if MIXER[layer] == 0:
                phase_rwkv_project(nc, g, layer, j)
                phase_rwkv_lora(nc, g, j)
                phase_scan(nc, g, j)
                phase_rwkv_finish(nc, g, j)
            elif MIXER[layer] == 1:
                phase_attention_project(nc, g)
                phase_attention(nc, g)
            else:
                phase_conv(nc, g)
            phase_output(nc, g, layer)
        phase_end(nc, g)


CHAN = {}


def chan_layout():
    if CHAN:
        return CHAN
    at = 0
    for name, n in (("norm_pre", 32), ("norm_post", 32), ("b_ada", 96), ("mu", 96), ("decay0", 32), ("icl0", 32),
                    ("k_k", 16), ("r_k", 16), ("gn_w", 16), ("gn_b", 16), ("k_a", 16), ("q_norm", 1), ("k_norm", 1),
                    ("conv_w", 24), ("conv_b", 8)):
        CHAN[name] = at
        at += n
    CHAN["_"] = at
    return CHAN


def ch(g, name, i, n=1):
    at = chan_layout()[name] + i
    return g.chan[:, at:at + n]


def slot_view(ps_banks):
    return ps_banks[:, :, 0:CW]


def as3(ap):
    return ap.rearrange("p (c n) -> p c n", c=CH)


class Sems:

    def __init__(self, nc, ctx):
        self.nc, self.taken = nc, []
        Sems.phases += 1
        ctx.callback(self.release)

    phases = 0

    def release(self):
        self.nc.clear_and_free_semaphores(self.taken)
        self.nc.all_engine_barrier()

    def __call__(self, *names):
        got = [self.nc.alloc_semaphore(f"{n}_{Sems.phases}") for n in names]
        self.taken += got
        return got[0] if len(got) == 1 else got


def phase_start(nc, g):
    io = g.io
    c = chan_layout()
    with ExitStack() as ctx:
        sem = Sems(nc, ctx)
        loaded, ident_in, cond_ok, sig_ok, silu_ok, rows_mm, rows_sb, cols_mm, cols_sb, vec_ok, set_ok = sem(
            "loaded", "ident_in", "cond_in", "sig_ok", "silu_ok", "rows_mm", "rows_sb", "cols_mm", "cols_sb", "vec_ok", "set_ok")
        SLOTS = 6
        wa_in = [sem(f"wa_in{i}") for i in range(SLOTS)]
        wsz = NB * 512
        wa = [g.arena[:, i * wsz:(i + 1) * wsz].rearrange("p (k n) -> p k n", k=NB) for i in range(SLOTS)]
        at = SLOTS * wsz
        rows = g.arena[0:2, at:at + 3072]
        at += 3072
        cond = g.arena[:, at:at + 16].rearrange("p (k c) -> p k c", c=2)
        sig = g.arena[:, at + 16:at + 32].rearrange("p (k c) -> p k c", c=2)
        silu = g.arena[:, at + 32:at + 48].rearrange("p (k c) -> p k c", c=2)
        block = ctx.enter_context(nc.Block())

        @block.sync
        def _(sp):
            sp.dma_start(cond, io["cond"]).then_inc(cond_ok, 16)
            sp.dma_start(g.ident[:, :], io["ident"]).then_inc(ident_in, 16)

            def slab(n, s):
                sp.dma_start(wa[s], io["w_ada"][bass.ds(n, 1)].rearrange("o p k n -> (o p) k n")).then_inc(wa_in[s], 16)

            for n in range(SLOTS):
                slab(n, n)
            sp.dma_start(g.chan[:, :], io["chan"]).then_inc(loaded, 16)
            sp.dma_start(g.x[:, :, :], io["x"]).then_inc(loaded, 16)
            sp.dma_start(g.ones[:, :], io["ones"]).then_inc(loaded, 16)
            sp.dma_start(g.head_ones[:, :], io["head_ones"]).then_inc(loaded, 16)
            with sp.Fori(1, 24 // SLOTS) as i:
                for s in range(SLOTS):
                    sp.wait_ge(rows_mm, SLOTS * i + s - SLOTS + 1)
                    slab(SLOTS * i + s, s)
            sp.wait_ge(loaded, 64)

        @block.scalar
        def _(act):
            act.wait_ge(cond_ok, 16)
            nc.scalar.activation(sig, cond, ACT.Sigmoid).then_inc(sig_ok, 1)
            for layer in range(4):
                for q in range(6):
                    act.wait_ge(rows_mm, 6 * layer + q + 1)
                    if q == 0 and layer:
                        act.wait_ge(cols_mm, layer)
                    nc.scalar.copy(rows[:, q * 512:(q + 1) * 512], g.ps[0:2, q % 2, :]).then_inc(rows_sb, 1)

        @block.tensor
        def _(pe):
            pe.wait_ge(silu_ok, 1)
            pe.wait_ge(ident_in, 16)
            for layer in range(4):
                for q in range(6):
                    n = 6 * layer + q
                    pe.wait_ge(wa_in[n % SLOTS], 16 * (n // SLOTS + 1))
                    if n >= 2:
                        pe.wait_ge(rows_sb, n - 1)
                    for k in range(NB):
                        mm = pe.matmul(g.ps[0:2, n % 2, :], silu[:, k, :], wa[n % SLOTS][:, k, :], start=k == 0, stop=k == NB - 1)
                    mm.then_inc(rows_mm, 1)
                pe.wait_ge(rows_sb, 6 * layer + 6)
                if layer:
                    pe.wait_ge(cols_sb, layer)
                for b in range(24):
                    mm = pe.transpose(g.ps[:, 2, 2 * b:2 * b + 2], rows[:, b * P:(b + 1) * P], g.ident[0:2, 0:2])
                mm.then_inc(cols_mm, 1)

        @block.vector
        def _(dve):
            nc.vector.memset(g.eps[:, :], GN_EPS).then_inc(set_ok, 1)
            nc.vector.memset(g.flag[:, :], 0.0).then_inc(set_ok, 1)
            dve.wait_ge(set_ok, 2)
            dve.wait_ge(sig_ok, 1)
            nc.vector.tensor_tensor(silu, cond, sig, op=ALU.mult).then_inc(silu_ok, 1)
            dve.wait_ge(loaded, 64)
            k = 0
            for layer in range(4):
                a = g.ada[:, layer]
                dve.wait_ge(cols_mm, layer + 1)
                b0 = c["b_ada"] + 24 * layer
                bias = g.chan[:, b0:b0 + 24].rearrange("p (n o) -> p n o", o=1).to_broadcast([P, 24, 2])
                nc.vector.tensor_tensor(a, g.ps[:, 2, 0:48].rearrange("p (n c) -> p n c", c=2), bias, op=ALU.add).then_inc(cols_sb, 1)
                dve.wait_ge(cols_sb, layer + 1)
                n0 = c["norm_pre"] + 8 * layer
                pre = g.chan[:, n0:n0 + 8].rearrange("p (n o) -> p n o", o=1).to_broadcast([P, 8, 2])
                n1 = c["norm_post"] + 8 * layer
                post = g.chan[:, n1:n1 + 8].rearrange("p (n o) -> p n o", o=1).to_broadcast([P, 8, 2])
                nc.vector.scalar_tensor_tensor(a[:, 8:16, :], a[:, 8:16, :], 1.0, pre, op0=ALU.add, op1=ALU.mult).then_inc(vec_ok, 1)
                nc.vector.tensor_tensor(a[:, 16:24, :], a[:, 16:24, :], post, op=ALU.mult).then_inc(vec_ok, 1)
                k += 2
            dve.wait_ge(vec_ok, k)


def token_ranges():
    return ((0, 0, CTX), (1, CTX, T))


def norm_matmuls(pe, g, sq, sq_ok, used, banks):
    for b in range(NB):
        pe.wait_ge(sq_ok, b + 1)
        for c in range(CH):
            mm = pe.matmul(g.ps[:, banks + c, 0:CW], g.ones[:, :], sq[b % 2][:, c * CW:(c + 1) * CW],
                           start=b == 0, stop=b == NB - 1)
        mm.then_inc(used, 1)


def phase_prenorm(nc, g, layer):
    h = g.big[0]
    tmp = g.big[1]
    sq = [g.big[2][:, i, :] for i in range(2)]
    ms, root, rstd = g.big[2][:, 2, :], g.big[2][:, 3, :], g.big[2][:, 4, :]
    ada = g.ada[:, layer]
    with ExitStack() as ctx:
        sem = Sems(nc, ctx)
        sq_ok, sq_used, ms_ok, root_ok, rstd_ok, tmp_ok, h_ok = sem("sq_ok", "sq_used", "ms_ok", "root_ok", "rstd_ok", "tmp_ok", "h_ok")
        block = ctx.enter_context(nc.Block())

        @block.scalar
        def _(act):
            for b in range(NB):
                if b >= 2:
                    act.wait_ge(sq_used, b - 1)
                nc.scalar.activation(sq[b % 2], g.x[:, b, :], ACT.Square).then_inc(sq_ok, 1)
            act.wait_ge(ms_ok, 1)
            nc.scalar.activation(root, ms, ACT.Ln).then_inc(root_ok, 1)
            act.wait_ge(root_ok, 1)
            nc.scalar.activation(rstd, root, ACT.Exp, scale=-0.5).then_inc(rstd_ok, 1)
            for b in range(NB):
                act.wait_ge(tmp_ok, b + 1)
                for c, a0, a1 in token_ranges():
                    nc.scalar.activation(h[:, b, a0:a1], tmp[:, b, a0:a1], ACT.Identity, bias=ada[:, b, c:c + 1],
                                         scale=ada[:, 8 + b, c:c + 1]).then_inc(h_ok, 1)
            act.wait_ge(h_ok, 2 * NB)

        @block.tensor
        def _(pe):
            norm_matmuls(pe, g, sq, sq_ok, sq_used, 0)

        @block.vector
        def _(dve):
            dve.wait_ge(sq_used, NB)
            nc.vector.tensor_scalar(as3(ms), slot_view(g.ps[:, 0:3, :]), 1.0 / D, RMS_EPS, ALU.mult, ALU.add).then_inc(ms_ok, 1)
            dve.wait_ge(rstd_ok, 1)
            for b in range(NB):
                nc.vector.tensor_tensor(tmp[:, b, :], g.x[:, b, :], rstd, op=ALU.mult).then_inc(tmp_ok, 1)
            dve.wait_ge(tmp_ok, NB)


def load_slabs(sp, g, first, count, slab_in, proj_done, n0=0):
    def one(n, s, free=True):
        if free:
            sp.wait_ge(proj_done, n - WSLOTS + 1)
        src = g.io["w"][bass.ds(first - n0 + n, 1)].rearrange("o p k -> (o p) k")
        sp.dma_start(g.slab[:, s, :], src).then_inc(slab_in[s], 16)

    n = n0
    end = n0 + count
    while n < end and n < WSLOTS:
        one(n, n % WSLOTS, free=False)
        n += 1
    groups = (end - n) // WSLOTS
    if groups > 1:
        with sp.Fori(0, groups) as i:
            for u in range(WSLOTS):
                one(n + u + WSLOTS * i, (n + u) % WSLOTS)
        n += WSLOTS * groups
    while n < end:
        one(n, n % WSLOTS)
        n += 1


def multiply(pe, g, rhs, slot, bank, done):
    for k in range(NB):
        for c in range(CH):
            mm = pe.matmul(g.ps[:, bank + c, 0:CW], g.slab[:, slot, k * P:(k + 1) * P], rhs[:, k, c * CW:(c + 1) * CW],
                           start=k == 0, stop=k == NB - 1)
    mm.then_inc(done, 1)




def take_high(nc, dst, src):
    return nc.vector.tensor_copy(dst, src)


def high_slab(nc, g, dve, n, slab_in, proj_done, high_ok):
    dve.wait_ge(slab_in[n % WSLOTS], 16 * (n // WSLOTS + 1))
    if n >= WSLOTS:
        dve.wait_ge(proj_done, n - WSLOTS + 1)
    take_high(nc, g.stage_r[:, n % WSLOTS, 0:D], g.slab[:, n % WSLOTS]).then_inc(high_ok, 1)


def split_slabs(nc, g, pool, count, high_ok, low_ok):
    with pool.Fori(0, count // WSLOTS) as i:
        for s in range(WSLOTS):
            pool.wait_ge(high_ok, WSLOTS * i + s + 1)
            nc.gpsimd.tensor_tensor(g.slab_r[:, s], g.slab[:, s], g.stage_r[:, s, 0:D], op=ALU.subtract).then_inc(low_ok, 1)


def split_rows(nc, g, dve, high, low, rows_high_ok, rows_ok):
    for k in range(NB):
        take_high(nc, g.big_r[high][:, k, :], g.big[low][:, k, :]).then_inc(rows_high_ok, 1)
        dve.wait_ge(rows_high_ok, k + 1)
        nc.vector.tensor_tensor(g.big_r[low][:, k, :], g.big[low][:, k, :], g.big_r[high][:, k, :], op=ALU.subtract).then_inc(rows_ok, 1)


def multiply_split(pe, g, high, low, slot, bank, done, rows_ok=None):
    w_high, w_low = g.stage_r[:, slot, 0:D], g.slab_r[:, slot]
    high, low = g.big_r[high], g.big_r[low]
    for k in range(NB):
        if rows_ok is not None:
            pe.wait_ge(rows_ok, k + 1)
        for i, (w, x) in enumerate(((w_high, high), (w_high, low), (w_low, high))):
            for c in range(CH):
                mm = pe.matmul(g.ps[:, bank + c, 0:CW], w[:, k * P:(k + 1) * P], x[:, k, c * CW:(c + 1) * CW],
                               start=k == i == 0, stop=k == NB - 1 and i == 2)
    mm.then_inc(done, 1)


def project(pe, g, rhs, count, n0, slab_in, evacuated, proj_done, split=None):
    def one(n, u):
        s = (n0 + u) % WSLOTS
        bank = 3 * ((n0 + u) % 2)
        if split:
            pe.wait_ge(split[2], n + 1)
        else:
            pe.wait_ge(slab_in[s], 16 * (n // WSLOTS + 1) if isinstance(n, int) else (n - s) * (16 // WSLOTS) + 16)
        if not isinstance(n, int) or n >= 2:
            pe.wait_ge(evacuated, n - 1)
        if split:
            multiply_split(pe, g, split[0], split[1], s, bank, proj_done, split[3] if isinstance(n, int) and n == 0 else None)
        else:
            multiply(pe, g, rhs, s, bank, proj_done)

    if count % WSLOTS == 0 and count > WSLOTS and n0 >= 0:
        start = 0
        if n0 < 2:
            for u in range(WSLOTS):
                one(n0 + u, u)
            start = 1
        if count // WSLOTS - start > 1:
            with pe.Fori(start, count // WSLOTS) as i:
                for u in range(WSLOTS):
                    one(n0 + u + WSLOTS * i, u)
        else:
            for u in range(WSLOTS * start, count):
                one(n0 + u, u)
    else:
        for u in range(count):
            one(n0 + u, u)


W_RWKV = 34


def w_base(name, j=0):
    if name == "rwkv":
        return j * (W_RWKV + NB)
    at = 2 * (W_RWKV + NB)
    if name == "attn":
        return at
    at += 18 + NB
    return at


def phase_rwkv_project(nc, g, layer, j):
    h, xx, xs = g.big[0], g.big[1], [g.big[2], g.big[3]]
    lora = [g.big[0][:, 0, :], g.big[0][:, 1, :]]
    base = w_base("rwkv", j)
    with ExitStack() as ctx:
        sem = Sems(nc, ctx)
        half_ok, xx_ok, xs_ok, proj_done, evacuated = sem("half_ok", "xx_ok", "xs_ok", "proj_done", "evacuated")
        slab_in = [sem(f"slab_in{i}") for i in range(WSLOTS)]
        stored = [sem(f"stored{i}") for i in range(2)]
        block = ctx.enter_context(nc.Block())
        ranges = token_ranges()

        @block.sync
        def _(sp):
            load_slabs(sp, g, base, W_RWKV, slab_in, proj_done)

        @block.tensor
        def _(pe):
            for m in range(4):
                pe.wait_ge(xs_ok, NB * (m + 1))
                project(pe, g, xs[m % 2], NB, NB * m, slab_in, evacuated, proj_done)
            for m in (4, 5):
                pe.wait_ge(xs_ok, NB * (m + 1))
                project(pe, g, xs[m % 2], 1, 32 + m - 4, slab_in, evacuated, proj_done)

        @block.scalar
        def _(act):
            for m in range(4):
                arr = (A_R, A_K, A_V, A_G)[m]
                for b in range(NB):
                    n = NB * m + b
                    act.wait_ge(proj_done, n + 1)
                    if n >= 2:
                        act.wait_ge(stored[n % 2], 16 * (n // 2))
                    st = g.stage[:, n % 2, :]
                    nc.scalar.copy(as3(st), slot_view(g.ps[:, 3 * (n % 2):3 * (n % 2) + 3, :])).then_inc(evacuated, 1)
                    act.wait_ge(evacuated, n + 1)
                    dst = g.scan_in[b::NB, arr].rearrange("t p n -> p t n")
                    act.dma_start(dst, st.rearrange("p (t n) -> p t n", n=P)).then_inc(stored[n % 2], 16)
            act.wait_ge(xs_ok, 6 * NB)
            for m in (4, 5):
                n = 32 + m - 4
                act.wait_ge(proj_done, n + 1)
                fn = ACT.Tanh if m == 4 else ACT.Copy
                nc.scalar.activation(as3(lora[m - 4]), slot_view(g.ps[:, 3 * (n % 2):3 * (n % 2) + 3, :]), fn).then_inc(evacuated, 1)
            act.wait_ge(evacuated, 34)
            for s in range(2):
                act.wait_ge(stored[s], 16 * 16)

        @block.vector
        def _(dve):
            for b in range(NB):
                for _, a0, a1 in ranges:
                    nc.vector.tensor_tensor(xx[:, b, a0 + 1:a1 - 1], h[:, b, a0:a1 - 2], h[:, b, a0 + 2:a1], op=ALU.add).then_inc(half_ok, 1)
                    nc.vector.tensor_copy(xx[:, b, a0:a0 + 1], h[:, b, a0 + 1:a0 + 2]).then_inc(half_ok, 1)
                    nc.vector.tensor_copy(xx[:, b, a1 - 1:a1], h[:, b, a1 - 2:a1 - 1]).then_inc(half_ok, 1)
            for b in range(NB):
                dve.wait_ge(half_ok, 6 * (b + 1))
                nc.vector.scalar_tensor_tensor(xx[:, b, :], xx[:, b, :], 0.5, h[:, b, :], op0=ALU.mult, op1=ALU.subtract).then_inc(xx_ok, 1)
            for m in range(6):
                if m >= 2:
                    dve.wait_ge(proj_done, NB * (m - 1))
                for b in range(NB):
                    if m == 0:
                        dve.wait_ge(xx_ok, b + 1)
                    mu = ch(g, "mu", 48 * j + 8 * m + b)
                    nc.vector.scalar_tensor_tensor(xs[m % 2][:, b, :], xx[:, b, :], mu, h[:, b, :], op0=ALU.mult, op1=ALU.add).then_inc(xs_ok, 1)
            dve.wait_ge(xs_ok, 6 * NB)


def phase_rwkv_lora(nc, g, j):
    lora = [g.big[0][:, 0, :], g.big[0][:, 1, :]]
    up = g.big[1][:, 0:4, :].rearrange("p b t -> p (b t)")[:, 0:2 * 16 * P].rearrange("p (m n) -> p m n", n=P)
    keys = [g.big[2][:, i, :] for i in range(2)]
    kc = [g.big[2][:, 2 + i, :] for i in range(2)]
    sq = [g.big[2][:, 4 + i, :] for i in range(2)]
    root = [g.big[2][:, 6 + i, :] for i in range(2)]
    inv = [g.big[3][:, i, :] for i in range(2)]
    with ExitStack() as ctx:
        sem = Sems(nc, ctx)
        up_in, up_mm, up_sb, kc_ok, sq_ok, norm_mm, root_ok, clamp_ok, inv_ok, kk_ok = sem(
            "up_in", "up_mm", "up_sb", "kc_ok", "sq_ok", "norm_mm", "root_ok", "clamp_ok", "inv_ok", "kk_ok")
        key_in = [sem(f"key_in{i}") for i in range(2)]
        stored = [sem(f"stored{i}") for i in range(2)]
        kk_stored = [sem(f"kk_stored{i}") for i in range(2)]
        block = ctx.enter_context(nc.Block())
        bank = lambda b, k: 3 * ((5 * b + k) % 2)

        @block.sync
        def _(sp):
            sp.dma_start(up, g.io["lora_up"][j]).then_inc(up_in, 16)
            for b in range(NB):
                if b >= 2:
                    sp.wait_ge(kc_ok, b - 1)
                sp.dma_start(keys[b % 2].rearrange("p (t n) -> p t n", n=P),
                             g.scan_in[b::NB, A_K].rearrange("t p n -> p t n")).then_inc(key_in[b % 2], 16)
                if b >= 1:
                    q = b - 1
                    sp.wait_ge(kk_ok, q + 1)
                    sp.dma_start(g.scan_in[q::NB, A_KK].rearrange("t p n -> p t n"),
                                 inv[q % 2].rearrange("p (t n) -> p t n", n=P)).then_inc(kk_stored[q % 2], 16)
            q = NB - 1
            sp.wait_ge(kk_ok, q + 1)
            sp.dma_start(g.scan_in[q::NB, A_KK].rearrange("t p n -> p t n"),
                         inv[q % 2].rearrange("p (t n) -> p t n", n=P)).then_inc(kk_stored[q % 2], 16)
            for s in range(2):
                sp.wait_ge(kk_stored[s], 64)

        @block.tensor
        def _(pe):
            pe.wait_ge(up_in, 16)

            def rates(b):
                for z in range(2):
                    for w in range(2):
                        n = 4 * b + 2 * z + w
                        if 2 * z + w == 1 and b:
                            pe.wait_ge(clamp_ok, b)
                        elif 2 * z + w != 1 and n:
                            pe.wait_ge(up_sb, n if 2 * z + w == 0 else n - 1)
                        for c in range(CH):
                            mm = pe.matmul(g.ps[:, bank(b, 2 * z + w) + c, 0:CW], up[:, (w * 2 + z) * NB + b, :],
                                           lora[w][:, c * CW:(c + 1) * CW], start=True, stop=True)
                        mm.then_inc(up_mm, 1)

            for b in range(NB):
                rates(b)
                pe.wait_ge(sq_ok, b + 1)
                pe.wait_ge(up_sb, 4 * b + 3)
                for c in range(CH):
                    mm = pe.matmul(g.ps[:, bank(b, 4) + c, 0:CW], g.head_ones[:, :], sq[b % 2][:, c * CW:(c + 1) * CW], start=True, stop=True)
                mm.then_inc(norm_mm, 1)

        @block.scalar
        def _(act):
            for b in range(NB):
                for z in range(2):
                    for w in range(2):
                        n = 4 * b + 2 * z + w
                        act.wait_ge(up_mm, n + 1)
                        if n >= 2:
                            act.wait_ge(stored[n % 2], 16 * (n // 2))
                        st = g.stage[:, n % 2, :]
                        bias = ch(g, "icl0" if w else "decay0", 16 * j + 8 * z + b)
                        bk = bank(b, 2 * z + w)
                        nc.scalar.activation(as3(st), slot_view(g.ps[:, bk:bk + 3, :]), ACT.Sigmoid, bias=bias).then_inc(up_sb, 1)
                        act.wait_ge(up_sb, n + 1)
                        arr = ((A_SW0, A_A0), (A_SW1, A_A1))[z][w]
                        act.dma_start(g.scan_in[b::NB, arr].rearrange("t p n -> p t n"),
                                      st.rearrange("p (t n) -> p t n", n=P)).then_inc(stored[n % 2], 16)
                act.wait_ge(clamp_ok, b + 1)
                nc.scalar.activation(root[b % 2], root[b % 2], ACT.Ln).then_inc(root_ok, 1)
                act.wait_ge(root_ok, b + 1)
                if b >= 2:
                    act.wait_ge(kk_stored[b % 2], 16 * (b // 2))
                nc.scalar.activation(inv[b % 2], root[b % 2], ACT.Exp, scale=-0.5).then_inc(inv_ok, 1)
            for s in range(2):
                act.wait_ge(stored[s], 16 * 16)

        @block.vector
        def _(dve):
            def scaled(b):
                dve.wait_ge(key_in[b % 2], 16 * (b // 2 + 1))
                if b >= 2:
                    dve.wait_ge(kk_ok, b - 1)
                nc.vector.tensor_scalar(kc[b % 2], keys[b % 2], ch(g, "k_k", 8 * j + b), None, ALU.mult).then_inc(kc_ok, 1)
                dve.wait_ge(kc_ok, b + 1)
                if b >= 2:
                    dve.wait_ge(norm_mm, b - 1)
                nc.vector.tensor_tensor(sq[b % 2], kc[b % 2], kc[b % 2], op=ALU.mult).then_inc(sq_ok, 1)

            scaled(0)
            for b in range(NB):
                if b + 1 < NB:
                    scaled(b + 1)
                dve.wait_ge(norm_mm, b + 1)
                if b >= 2:
                    dve.wait_ge(inv_ok, b - 1)
                bk = bank(b, 4)
                nc.vector.tensor_scalar(as3(root[b % 2]), slot_view(g.ps[:, bk:bk + 3, :]), 1e-24, None, ALU.max).then_inc(clamp_ok, 1)
                dve.wait_ge(inv_ok, b + 1)
                nc.vector.tensor_tensor(inv[b % 2], inv[b % 2], kc[b % 2], op=ALU.mult).then_inc(kk_ok, 1)


PAIRS = NT * NB // 2
CTX_PAIRS = NB // 2
MASKS = {name: i for i, name in enumerate(("strict", "incl", "lv0t", "lv1", "lv2", "lv3", "lv4", "lv5", "eye"))}


def phase_scan(nc, g, j):
    io = g.io
    at = [0]

    def take(*shape):
        n = int(np.prod(shape))
        ap = g.arena[:, at[0]:at[0] + n]
        at[0] += n
        assert at[0] <= 4 * NB * T
        names = "abcd"[:len(shape)]
        if len(shape) == 1:
            return ap
        return ap.rearrange("p (%s) -> p %s" % (" ".join(names), " ".join(names)), **dict(zip(names, shape)))

    raw = [take(6, 4, P) for _ in range(2)]
    ka = [take(4) for _ in range(2)]
    wA, wR = [[take(4, P) for _ in range(2)] for _ in range(2)]
    wB, wK = [[[take(4, P) for _h in range(2)] for _ in range(2)] for _ in range(2)]
    inv_t, tak_t, trb_t, trk_t = [[[take(4, P) for _h in range(2)] for _ in range(2)] for _ in range(4)]
    tokB, tokK, tokV = [[take(4, P) for _ in range(2)] for _ in range(3)]
    tab_t, X, XT, U = [[take(4, P) for _h in range(2)] for _ in range(4)]
    cum, d1, d0, kd, bb, eA, eR, eB = [take(4, P) for _ in range(8)]
    masks = take(len(MASKS), 2, P)
    reset = take(4 * P)
    f_in, f_out = [[take(4) for _ in range(2)] for _ in range(2)]
    rhs_sb, sa_sb, hs = take(4, P), take(4, P), take(4, P)
    hn = take(4, HD)
    stage = g.stage[:, :, :].rearrange("p a b -> p (a b)")
    ystage = [stage[:, i * 512:(i + 1) * 512].rearrange("p (a b) -> p a b", a=4) for i in range(2)]
    hin = [stage[:, 1024 + i * 256:1280 + i * 256].rearrange("p (a b) -> p a b", a=4) for i in range(2)]
    hout = [stage[:, 1536 + i * 256:1792 + i * 256].rearrange("p (a b) -> p a b", a=4) for i in range(2)]

    def mask(name):
        return masks[:, MASKS[name]].rearrange("p (o d) n -> p o d n", o=1).to_broadcast([P, 2, 2, P])

    def sd(ap):
        return ap.rearrange("p (s d) n -> p s d n", s=2)

    def bank(i):
        return g.ps[:, i, :].rearrange("p (a n) -> p a n", a=4)

    b_u, b_x, b_xt = [[bank(2 * i), bank(2 * i + 1)] for i in range(3)]
    b_rhs, b_sa = bank(6), bank(7)
    bk_rhs, bk_sa = [g.ps[:, 6 + i, :].rearrange("p (t a n) -> p t a n", t=2, a=4) for i in range(2)]
    bk_rhs, bk_sa = [[bk[:, t] for t in range(2)] for bk in (bk_rhs, bk_sa)]
    b_st = g.ps[:, 6, 0:256].rearrange("p (a n) -> p a n", a=4)
    rows = [slice(0, HD), slice(HD, P)]
    cols = rows
    V = nc.vector

    with ExitStack() as ctx:
        sem = Sems(nc, ctx)
        const_in, init_in, scan_ok, d1_ok, d0_ok, exp_ok, fac_ok, t_ok, kd_ok, b_ok, w_ok, wp_ok = sem(
            "const_in", "init_in", "scan_ok", "d1_ok", "d0_ok", "exp_ok", "fac_ok", "t_ok", "kd_ok", "b_ok", "w_ok", "wp_ok")
        gram_mm, x1_mm, u_mm, x_mm, t_mm, f_mm, late_mm, tok_mm = sem(
            "gram_mm", "x1_mm", "u_mm", "x_mm", "t_mm", "f_mm", "late_mm", "tok_mm")
        zero_ok, zero_k_ok, tab_ok, x0_ok, eye_ok, x1_ok, u_ok, xa_ok, xt_ok, u6_ok, inv_ok, late_ok, tok_ok = sem(
            "zero_ok", "zero_k_ok", "tab_ok", "x0_ok", "eye_ok", "x1_ok", "u_ok", "xa_ok", "xt_ok", "u6_ok", "inv_ok", "late_ok", "tok_ok")
        rhs_mm, sa_mm, st_mm, y_mm, rhs_ok, sa_ok, y_ok, hs_ok, hn_ok, ho_ok = sem(
            "rhs_mm", "sa_mm", "st_mm", "y_mm", "rhs_ok", "sa_ok", "y_ok", "hs_ok", "hn_ok", "ho_ok")
        raw_in, hin_in, y_stored, h_stored = [[sem(f"{n}{i}") for i in range(2)] for n in ("raw_in", "hin_in", "y_stored", "h_stored")]
        block = ctx.enter_context(nc.Block())

        def each_pair(eng, fn):
            for q in range(6):
                fn(q, q % 2, q // 2)
            with eng.Fori(3, PAIRS // 2 - 1) as i:
                for p in range(2):
                    fn(2 * i + p, p, i)
            for q in range(PAIRS - 2, PAIRS):
                fn(q, q % 2, q // 2)

        known = lambda q: isinstance(q, int)

        @block.sync
        def _(sp):
            sp.dma_start(masks, io["masks"]).then_inc(const_in, 16)
            sp.dma_start(reset, io["reset"]).then_inc(const_in, 16)
            sp.dma_start(g.state[0:NB], io["state_in"][j]).then_inc(init_in, 16)

            def load_raw(q, p, i):
                for s in range(2):
                    n = 2 * q + s
                    back = (NB - 1 - n) if known(q) and q < CTX_PAIRS else ((NT + 1) * NB - 1) - n
                    f = lambda a0, a1, m: g.scan_in[bass.ds(m, 1), a0:a1].rearrange("o a p t -> p (o a) t")
                    sp.dma_start(raw[p][:, 0:6, 2 * s, :], f(A_SW0, A_V + 1, n)).then_inc(raw_in[p], 16)
                    sp.dma_start(raw[p][:, 2:6, 2 * s + 1, :], f(A_R, A_V + 1, back)).then_inc(raw_in[p], 16)
                    sp.dma_start(raw[p][:, 0:2, 2 * s + 1, :], f(A_SW1, A_A1 + 1, back)).then_inc(raw_in[p], 16)
                sp.dma_start(ka[p], io["ka"][j][bass.ds(q, 1)].rearrange("o p n -> (o p) n")).then_inc(raw_in[p], 16)

            load_raw(0, 0, 0)

            def pair(q, p, i):
                if not known(q) or q + 1 < PAIRS:
                    if not known(q) or q >= 1:
                        sp.wait_ge(tok_mm, 3 * q)
                    sp.wait_ge(init_in, 16)
                    load_raw(q + 1, 1 - p, 0)
                if not known(q) or q >= CTX_PAIRS:
                    sp.wait_ge(hs_ok, 2 * (q - 1))
                    sp.wait_ge(init_in, 16)
                    if not known(q) or q >= 2 * CTX_PAIRS:
                        sp.wait_ge(h_stored[p], 16 * i - 16)
                    sp.wait_ge(init_in, 16)
                    for_slot = 2 * q - NB
                    sp.dma_start(hin[p].rearrange("p (s d) n -> p s d n", s=2),
                                 g.state[bass.ds(for_slot, 2)].rearrange("s p d n -> p s d n")).then_inc(hin_in[p], 16)
            each_pair(sp, pair)

        @block.tensor
        def _(pe):
            U4 = range(4)

            def chain_rhs(c, p):
                pe.wait_ge(hs_ok, 2 * c + 2)
                pe.wait_ge(hn_ok, 2 * c)
                pe.wait_ge(tok_ok, 3 * c + 3)
                for u in U4:
                    pe.matmul(b_rhs[:, u, :], wA[p][:, u, :], hs[:, u, :], start=True, stop=False)
                    for z in range(2):
                        for h in range(2):
                            mm = pe.matmul(b_rhs[rows[z], u, cols[h]], tak_t[p][h][:, u, cols[z]], tokV[p][:, u, cols[h]],
                                           start=False, stop=h == 1)
                mm.then_inc(rhs_mm, 1)

            def chain_sa(c, p):
                pe.wait_ge(rhs_ok, c + 1)
                for u in U4:
                    for h in range(2):
                        for z in range(2):
                            mm = pe.matmul(b_sa[rows[z], u, cols[h]], inv_t[p][h][:, u, cols[z]], rhs_sb[:, u, cols[h]],
                                           start=True, stop=True)
                mm.then_inc(sa_mm, 1)

            def chain_state(c, p):
                pe.wait_ge(sa_ok, c + 1)
                for u in U4:
                    for h in range(2):
                        pe.matmul(b_st[rows[h], u, :], tokB[p][:, u, cols[h]], sa_sb[:, u, cols[h]], start=True, stop=False)
                        mm = pe.matmul(b_st[rows[h], u, :], tokK[p][:, u, cols[h]], tokV[p][:, u, cols[h]], start=False, stop=True)
                mm.then_inc(st_mm, 1)

            def chain_y(c, p):
                for u in U4:
                    pe.matmul(b_sa[:, u, :], hs[:, u, :], wR[p][:, u, :], start=True, stop=False)
                    for h in range(2):
                        out = b_sa[rows[h], u, :]
                        pe.matmul(out, sa_sb[:, u, cols[h]], trb_t[p][h][:, u, :], start=False, stop=False)
                        mm = pe.matmul(out, tokV[p][:, u, cols[h]], trk_t[p][h][:, u, :], start=False, stop=True)
                mm.then_inc(y_mm, 1)

            def tok_head(bk, p, h):
                for t, src in enumerate((wB, wK)):
                    for u in U4:
                        mm = pe.transpose(bk[t][:, u, :], src[p][h][rows[h], u, :], g.ident[rows[h], cols[h]])
                mm.then_inc(tok_mm, 1)

            def pair(q, p, i):
                chain = not known(q) or q >= 1
                c = q - 1
                pe.wait_ge(w_ok, 3 * q + 3)
                for h in range(2):
                    if chain:
                        pe.wait_ge(late_ok, 6 * q - 4 + h)
                    for u in U4:
                        mm = pe.matmul(b_u[h][:, u, :], wB[p][h][:, u, :], wA[p][:, u, :], start=True, stop=True)
                    mm.then_inc(gram_mm, 1)
                if chain:
                    chain_rhs(c, 1 - p)
                if chain:
                    pe.wait_ge(late_ok, 6 * q)
                for h in range(2):
                    pe.wait_ge(eye_ok, 2 * q + h + 1)
                    for u in U4:
                        mm = pe.transpose(b_x[h][:, u, :], XT[h][:, u, :], g.ident[:, :])
                    mm.then_inc(x1_mm, 1)
                if chain:
                    chain_sa(c, 1 - p)
                for k in range(1, LEVELS - 1):
                    for h in range(2):
                        if k == 1:
                            pe.wait_ge(x1_ok, 2 * q + h + 1)
                        else:
                            pe.wait_ge(xa_ok, 10 * q + 2 * (k - 2) + h + 1)
                        for u in U4:
                            mm = pe.matmul(b_u[h][:, u, :], tab_t[h][:, u, :], X[h][:, u, :], start=True, stop=True)
                        mm.then_inc(u_mm, 1)
                        if k == 5 and h == 1:
                            pe.wait_ge(wp_ok, 3 * q + 3)
                            if chain:
                                pe.wait_ge(y_ok, q)
                        if k > 1:
                            for u in U4:
                                mm = pe.transpose(b_xt[h][:, u, :], X[h][:, u, :], g.ident[:, :])
                            mm.then_inc(t_mm, 1)
                    if chain and k == 2:
                        chain_state(c, 1 - p)
                    if chain and k == 3:
                        chain_y(c, 1 - p)
                    if k == 4:
                        if chain:
                            pe.wait_ge(hn_ok, 2 * q)
                        for u in U4:
                            mm = pe.transpose(b_rhs[:, u, :], raw[p][:, R_V, u, :], g.ident[:, :])
                        mm.then_inc(tok_mm, 1)
                    if k == 5:
                        tok_head(bk_sa, p, 0)
                    for h in range(2):
                        pe.wait_ge(u_ok, 10 * q + 2 * (k - 1) + h + 1)
                        if k > 1:
                            pe.wait_ge(xt_ok, 10 * q + 2 * (k - 2) + h + 1)
                        for u in U4:
                            mm = pe.matmul(b_x[h][:, u, :], XT[h][:, u, :], U[h][:, u, :], start=True, stop=True)
                        mm.then_inc(x_mm, 1)
                for h in range(2):
                    pe.wait_ge(xa_ok, 10 * q + 8 + h + 1)
                    for u in U4:
                        d = u % 2
                        mm = pe.matmul(b_u[h][rows[1 - d], u, 0:HD], tab_t[h][:, u, cols[1 - d]], X[h][:, u, cols[d]], start=True, stop=True)
                    mm.then_inc(u_mm, 1)
                    if h == 1:
                        pe.wait_ge(tok_ok, 3 * q + 1)
                    for u in U4:
                        mm = pe.transpose(b_xt[h][:, u, :], X[h][:, u, :], g.ident[:, :])
                    mm.then_inc(t_mm, 1)
                tok_head(bk_rhs, p, 1)
                for h in range(2):
                    pe.wait_ge(u6_ok, 4 * q + 2 * h + 2)
                    pe.wait_ge(xt_ok, 10 * q + 8 + h + 1)
                    for u in U4:
                        d = u % 2
                        mm = pe.matmul(b_x[h][rows[d], u, 0:HD], U[h][:, u, 0:HD], inv_t[p][h][:, u, cols[1 - d]], start=True, stop=True)
                    mm.then_inc(f_mm, 1)
                for h in range(2):
                    for u in U4:
                        mm = pe.matmul(b_u[h][:, u, :], wK[p][h][:, u, :], wA[p][:, u, :], start=True, stop=True)
                    mm.then_inc(late_mm, 1)
                for h in range(2):
                    for u in U4:
                        mm = pe.matmul(b_xt[h][:, u, :], wB[p][h][:, u, :], wR[p][:, u, :], start=True, stop=True)
                    mm.then_inc(late_mm, 1)
                for h in range(2):
                    pe.wait_ge(inv_ok, 4 * q + 2 * h + 2)
                    for u in U4:
                        mm = pe.matmul(b_x[h][:, u, :], wK[p][h][:, u, :], wR[p][:, u, :], start=True, stop=True)
                    mm.then_inc(late_mm, 1)

            pe.wait_ge(const_in, 32)
            each_pair(pe, pair)
            c, p = PAIRS - 1, 1
            pe.wait_ge(late_ok, 6 * PAIRS)
            chain_rhs(c, p)
            chain_sa(c, p)
            chain_state(c, p)
            chain_y(c, p)

        @block.scalar
        def _(act):
            A = nc.scalar

            def chain_rhs(c):
                act.wait_ge(rhs_mm, c + 1)
                A.copy(rhs_sb, b_rhs).then_inc(rhs_ok, 1)

            def chain_sa(c):
                act.wait_ge(sa_mm, c + 1)
                A.copy(sa_sb, b_sa).then_inc(sa_ok, 1)

            def chain_out(c, p, i, ctx_pair):
                act.wait_ge(ho_ok, c + 1)
                n = 2 * c
                dst = (io["state_out"][j] if ctx_pair else g.state)[bass.ds(n, 2)].rearrange("s p d n -> p s d n")
                act.dma_start(dst, hout[p].rearrange("p (s d) n -> p s d n", s=2)).then_inc(h_stored[p], 16)

            def chain_y(c, p, i):
                act.wait_ge(y_mm, c + 1)
                act.wait_ge(y_stored[p], 16 * i)
                A.copy(ystage[p], b_sa).then_inc(y_ok, 1)
                act.wait_ge(y_ok, c + 1)
                n = 2 * c
                act.dma_start(g.scan_y[bass.ds(n, 2)].rearrange("s p d n -> p s d n"),
                              ystage[p].rearrange("p (s d) n -> p s d n", s=2)).then_inc(y_stored[p], 16)

            def exps(q, which=range(6)):
                act.wait_ge(d0_ok, q + 1)
                act.wait_ge(w_ok, 3 * q)
                act.wait_ge(wp_ok, 3 * q)
                s_ = -DECAY_SCALE
                todo = ((0, eB, d1, -s_), (1, eA, d1, -s_), (0, eR, d1, s_), (1, eB, d0, s_), (0, eA, d0, s_), (1, eR, d0, -s_))
                for e in which:
                    d, out, src, sign = todo[e]
                    A.activation(sd(out)[:, :, d, :], sd(src)[:, :, d, :], ACT.Exp, scale=sign).then_inc(exp_ok, 1)

            def factors(q, p):
                s_ = -DECAY_SCALE
                for d, out, src, col in ((0, f_in[p], cum, HD - 1), (1, f_out[p], cum, HD - 1), (0, f_out[p], d1, P - 1), (1, f_in[p], d1, P - 1)):
                    A.activation(out.rearrange("p (s d) -> p s d", s=2)[:, :, d], sd(src)[:, :, d, col], ACT.Exp, scale=s_).then_inc(fac_ok, 1)

            def tok(q, t, bk, dst):
                act.wait_ge(tok_mm, 3 * q + t + 1)
                A.copy(dst, bk).then_inc(tok_ok, 1)

            def tok_head(q, h, bk, p):
                act.wait_ge(tok_mm, 3 * q + h + 2)
                A.copy(tokB[p][:, :, cols[h]], bk[0])
                A.copy(tokK[p][:, :, cols[h]], bk[1]).then_inc(tok_ok, 1)

            exps(0)
            factors(0, 0)

            def pair(q, p, i):
                chain = not known(q) or q >= 1
                c = q - 1
                nxt = not known(q) or q + 1 < PAIRS
                ci = i - 1 if p == 0 else i
                if chain:
                    chain_rhs(c)
                for h in range(2):
                    act.wait_ge(x1_mm, 2 * q + h + 1)
                    A.copy(X[h], b_x[h]).then_inc(x1_ok, 1)
                if chain:
                    chain_sa(c)
                for k in range(2, LEVELS):
                    for h in range(2):
                        act.wait_ge(t_mm, 10 * q + 2 * (k - 2) + h + 1)
                        if k == LEVELS - 1:
                            for d in range(2):
                                A.copy(sd(U[h])[rows[1 - d], :, d, 0:HD], sd(b_u[h])[rows[1 - d], :, d, 0:HD]).then_inc(u6_ok, 1)
                        A.copy(XT[h] if k < LEVELS - 1 else inv_t[p][h], b_xt[h]).then_inc(xt_ok, 1)
                    if k == 2 and nxt:
                        exps(q + 1, range(2))
                    if k == 3:
                        if nxt:
                            exps(q + 1, range(2, 6))
                        if chain:
                            chain_y(c, 1 - p, ci)
                    if k == 4:
                        if chain:
                            chain_out(c, 1 - p, ci, known(q) and c < CTX_PAIRS)
                        if nxt:
                            factors(q + 1, 1 - p)
                        tok(q, 0, b_rhs, tokV[p])
                    if k == 5:
                        tok_head(q, 0, bk_sa, p)
                tok_head(q, 1, bk_rhs, p)
                for h in range(2):
                    act.wait_ge(f_mm, 2 * q + h + 1)
                    act.wait_ge(xt_ok, 10 * q + 8 + h + 1)
                    for d in range(2):
                        A.copy(sd(inv_t[p][h])[rows[d], :, d, cols[1 - d]], sd(b_x[h])[rows[d], :, d, 0:HD]).then_inc(inv_ok, 1)
            each_pair(act, pair)
            c = PAIRS - 1
            chain_rhs(c)
            chain_sa(c)
            chain_out(c, 1, PAIRS // 2 - 1, False)
            chain_y(c, 1, PAIRS // 2 - 1)
            for p in range(2):
                act.wait_ge(y_stored[p], 16 * (PAIRS // 2))
                act.wait_ge(h_stored[p], 16 * (PAIRS // 2))

        @block.vector
        def _(dve):
            def prep_decay(q, p, i):
                dve.wait_ge(raw_in[p], 112 * i + 112)
                dve.wait_ge(exp_ok, 6 * q)
                dve.wait_ge(fac_ok, 4 * q)
                flat = lambda a: a.rearrange("p a n -> p (a n)")
                V.tensor_tensor_scan(flat(cum), reset, raw[p][:, R_SW].rearrange("p a n -> p (a n)"), 0.0, op0=ALU.mult, op1=ALU.add).then_inc(scan_ok, 1)
                dve.wait_ge(scan_ok, q + 1)
                V.tensor_tensor(d1, cum, cum[:, :, HD - 1:HD].to_broadcast([P, 4, P]), op=ALU.subtract).then_inc(d1_ok, 1)
                dve.wait_ge(d1_ok, q + 1)
                V.tensor_tensor(d0, d1, raw[p][:, R_SW], op=ALU.subtract).then_inc(d0_ok, 1)

            def prep_k(q, p):
                dve.wait_ge(wp_ok, 3 * q)
                for u in range(4):
                    V.tensor_scalar(kd[:, u, :], raw[p][:, R_A, u, :], -1.0, ka[p][:, u:u + 1], ALU.add, ALU.mult).then_inc(t_ok, 1)
                dve.wait_ge(t_ok, 4 * q + 4)
                V.scalar_tensor_tensor(kd, kd, 1.0, raw[p][:, R_K], op0=ALU.add, op1=ALU.mult).then_inc(kd_ok, 1)

            def prep_ab(q, p):
                V.tensor_tensor(bb, raw[p][:, R_KK], raw[p][:, R_A], op=ALU.mult).then_inc(b_ok, 1)
                dve.wait_ge(exp_ok, 6 * q + 6)
                V.scalar_tensor_tensor(wA[p], raw[p][:, R_KK], -1.0, eA, op0=ALU.mult, op1=ALU.mult).then_inc(w_ok, 1)
                dve.wait_ge(b_ok, q + 1)
                for h in range(2):
                    V.tensor_tensor(wB[p][h][rows[h]], bb[rows[h]], eB[rows[h]], op=ALU.mult).then_inc(w_ok, 1)

            def wide(f, h):
                return f[rows[h]].rearrange("p (a n) -> p a n", n=1).to_broadcast([HD, 4, HD])

            def start_state(c, p, i, ctx_pair):
                dve.wait_ge(y_mm, c)
                dve.wait_ge(fac_ok, 4 * c + 4)
                if not ctx_pair:
                    dve.wait_ge(hin_in[p], 16 * (i - CTX_PAIRS // 2) + 16)
                for h in range(2):
                    if ctx_pair:
                        V.memset(hs[rows[h], :, cols[h]], 0.0).then_inc(hs_ok, 1)
                    else:
                        V.tensor_tensor(hs[rows[h], :, cols[h]], hin[p][rows[h]], wide(f_in[p], h), op=ALU.mult).then_inc(hs_ok, 1)

            def new_state(c, p, i):
                dve.wait_ge(hs_ok, 2 * c + 2)
                dve.wait_ge(ho_ok, c)
                dve.wait_ge(st_mm, c + 1)
                for h in range(2):
                    V.tensor_tensor(hn[rows[h]], b_st[rows[h]], hs[rows[h], :, cols[h]], op=ALU.add).then_inc(hn_ok, 1)
                dve.wait_ge(hn_ok, 2 * c + 2)
                dve.wait_ge(h_stored[p], 16 * i)
                V.tensor_tensor(hout[p], hn, f_out[p].rearrange("p (a n) -> p a n", n=1).to_broadcast([P, 4, HD]), op=ALU.mult).then_inc(ho_ok, 1)

            def pair(q, p, i):
                chain = not known(q) or q >= 1
                c = q - 1
                ci = (i - 1 if p == 0 else i)
                nxt = not known(q) or q + 1 < PAIRS
                for h in range(2):
                    dve.wait_ge(gram_mm, 2 * q + h + 1)
                    V.tensor_tensor(sd(tab_t[h]), sd(b_u[h]), mask("strict"), op=ALU.mult).then_inc(tab_ok, 1)
                    dve.wait_ge(tab_ok, 2 * q + h + 1)
                    V.tensor_tensor(sd(XT[h]), sd(tab_t[h]), mask("lv0t"), op=ALU.mult).then_inc(x0_ok, 1)
                    dve.wait_ge(x0_ok, 2 * q + h + 1)
                    V.tensor_tensor(sd(XT[h]), sd(XT[h]), mask("eye"), op=ALU.add).then_inc(eye_ok, 1)
                for k in range(1, LEVELS - 1):
                    for h in range(2):
                        dve.wait_ge(u_mm, 12 * q + 2 * (k - 1) + h + 1)
                        if k == 1:
                            dve.wait_ge(f_mm, 2 * q)
                        else:
                            dve.wait_ge(x_mm, 10 * q + 2 * (k - 2) + h + 1)
                        V.tensor_tensor(sd(U[h]), sd(b_u[h]), mask(f"lv{k}"), op=ALU.mult).then_inc(u_ok, 1)
                    for h in range(2):
                        dve.wait_ge(x_mm, 10 * q + 2 * (k - 1) + h + 1)
                        V.tensor_tensor(X[h], b_x[h], X[h], op=ALU.add).then_inc(xa_ok, 1)
                    if k == 1 and nxt:
                        prep_decay(q + 1, 1 - p, i if p == 0 else i + 1)
                    if k == 2 and nxt:
                        prep_k(q + 1, 1 - p)
                    if k == 3 and chain:
                        new_state(c, 1 - p, ci)
                    if k == 5 and nxt:
                        dve.wait_ge(y_mm, q)
                        prep_ab(q + 1, 1 - p)
                start_state(q, p, i, known(q) and q < CTX_PAIRS)
                for t, (bk, dst, m) in enumerate(((b_u, tak_t, "strict"), (b_xt, trb_t, "incl"), (b_x, trk_t, "incl"))):
                    for h in range(2):
                        dve.wait_ge(late_mm, 6 * q + 2 * t + h + 1)
                        V.tensor_tensor(sd(dst[p][h]), sd(bk[h]), mask(m), op=ALU.mult).then_inc(late_ok, 1)

            V.memset(hs, 0.0).then_inc(zero_ok, 1)
            for p in range(2):
                for h in range(2):
                    V.memset(wB[p][h], 0.0).then_inc(zero_ok, 1)
            dve.wait_ge(zero_ok, 5)
            dve.wait_ge(const_in, 32)
            prep_decay(0, 0, 0)
            prep_k(0, 0)
            prep_ab(0, 0)
            each_pair(dve, pair)
            new_state(PAIRS - 1, 1, PAIRS // 2 - 1)

        @block.gpsimd
        def _(pool):
            def prep(q, p):
                pool.wait_ge(kd_ok, q + 1)
                pool.wait_ge(exp_ok, 6 * q + 6)
                if not known(q) or q >= 2:
                    pool.wait_ge(y_mm, q - 1)
                for h in range(2):
                    nc.gpsimd.tensor_tensor(wK[p][h][rows[h]], kd[rows[h]], eB[rows[h]], op=ALU.mult).then_inc(wp_ok, 1)
                pool.wait_ge(wp_ok, 3 * q + 2)
                nc.gpsimd.tensor_tensor(wR[p], raw[p][:, R_R], eR, op=ALU.mult).then_inc(wp_ok, 1)

            for p in range(2):
                for h in range(2):
                    nc.gpsimd.memset(wK[p][h], 0.0).then_inc(zero_k_ok, 1)
            pool.wait_ge(zero_k_ok, 4)
            prep(0, 0)

            def pair(q, p, i):
                if not known(q) or q + 1 < PAIRS:
                    prep(q + 1, 1 - p)
            each_pair(pool, pair)


def phase_rwkv_finish(nc, g, j):
    og = g.big[0]
    load = [g.big[1], g.big[2]]
    YF, YB, RR, KK_, VV, GG, A0, A1 = range(8)
    t = g.big[3]
    asum, p = [t[:, i, :] for i in range(2)], [t[:, 2 + i, :] for i in range(2)]
    yy, root = t[:, 4, :], t[:, 5, :]
    sq, yn = t[:, 6, :], t[:, 7, :]
    sig, bonus = g.stage[:, 0, :], g.stage[:, 1, :]
    V, A = nc.vector, nc.scalar
    with ExitStack() as ctx:
        sem = Sems(nc, ctx)
        y_ok, mean_mm, yc_ok, sq_ok, var_mm, root_ok, inv_ok, yn_ok, ya_ok, as_ok, t_ok, kd_ok, p_ok, bonus_mm, bonus_ok, y2_ok, sig_ok, silu_ok, out_ok = sem(
            "y_ok", "mean_mm", "yc_ok", "sq_ok", "var_mm", "root_ok", "inv_ok", "yn_ok", "ya_ok", "as_ok", "t_ok", "kd_ok", "p_ok", "bonus_mm",
            "bonus_ok", "y2_ok", "sig_ok", "silu_ok", "out_ok")
        in_ = [sem(f"block_in{i}") for i in range(2)]
        block = ctx.enter_context(nc.Block())

        @block.sync
        def _(sp):
            for b in range(NB):
                if b >= 2:
                    sp.wait_ge(out_ok, b - 1)
                dst = lambda i: load[b % 2][:, i, :].rearrange("p (t n) -> p t n", n=P)
                sp.dma_start(dst(YF), g.scan_y[b::NB, :, 0].rearrange("t p n -> p t n")).then_inc(in_[b % 2], 16)
                sp.dma_start(dst(YB)[:, 0], g.scan_y[NB - 1 - b, :, 1]).then_inc(in_[b % 2], 16)
                for i in range(1, NT):
                    sp.dma_start(dst(YB)[:, i], g.scan_y[NB * (NT - i) + NB - 1 - b, :, 1]).then_inc(in_[b % 2], 16)
                for i, a in ((RR, A_R), (KK_, A_K), (VV, A_V), (GG, A_G), (A0, A_A0), (A1, A_A1)):
                    sp.dma_start(dst(i), g.scan_in[b::NB, a].rearrange("t p n -> p t n")).then_inc(in_[b % 2], 16)

        @block.tensor
        def _(pe):
            def heads(src, banks, done):
                for c in range(CH):
                    mm = pe.matmul(g.ps[:, banks + c, 0:CW] if banks < 6 else g.ps[:, 6, 0:CW], g.head_ones[:, :],
                                   src[:, c * CW:(c + 1) * CW], start=True, stop=True)
                mm.then_inc(done, 1)
            for b in range(NB):
                pe.wait_ge(y_ok, b + 1)
                if b:
                    pe.wait_ge(root_ok, b)
                heads(yy, 0, mean_mm)
                pe.wait_ge(p_ok, b + 1)
                if b:
                    pe.wait_ge(bonus_ok, b)
                heads(p[b % 2], 3, bonus_mm)
                pe.wait_ge(sq_ok, b + 1)
                heads(sq, 0, var_mm)

        @block.scalar
        def _(act):
            for b in range(NB):
                act.wait_ge(in_[b % 2], 256 * (b // 2 + 1))
                if b:
                    act.wait_ge(silu_ok, b)
                    act.wait_ge(out_ok, b)
                A.activation(sig, load[b % 2][:, GG, :], ACT.Sigmoid).then_inc(sig_ok, 1)
                act.wait_ge(yc_ok, b + 1)
                if b:
                    act.wait_ge(var_mm, b)
                A.activation(sq, yy, ACT.Square).then_inc(sq_ok, 1)
                act.wait_ge(var_mm, b + 1)
                if b:
                    act.wait_ge(yn_ok, b)
                A.activation(as3(root), slot_view(g.ps[:, 0:3, :]), ACT.Ln, bias=g.eps[:, 0:1], scale=1.0 / HD).then_inc(root_ok, 1)
                act.wait_ge(root_ok, b + 1)
                A.activation(root, root, ACT.Exp, scale=-0.5).then_inc(inv_ok, 1)

        @block.vector
        def _(dve):
            for b in range(NB):
                ld = load[b % 2]
                dve.wait_ge(in_[b % 2], 256 * (b // 2 + 1))
                if b:
                    dve.wait_ge(yn_ok, b)
                V.tensor_tensor(yy, ld[:, YF, :], ld[:, YB, :], op=ALU.add).then_inc(y_ok, 1)
                dve.wait_ge(as_ok, b + 1)
                V.tensor_scalar(asum[b % 2], asum[b % 2], -2.0, ch(g, "k_a", 8 * j + b), ALU.add, ALU.mult).then_inc(t_ok, 1)
                dve.wait_ge(t_ok, b + 1)
                V.scalar_tensor_tensor(asum[b % 2], asum[b % 2], 2.0, ld[:, KK_, :], op0=ALU.add, op1=ALU.mult).then_inc(kd_ok, 1)
                dve.wait_ge(kd_ok, b + 1)
                V.scalar_tensor_tensor(p[b % 2], asum[b % 2], ch(g, "r_k", 8 * j + b), ld[:, RR, :], op0=ALU.mult, op1=ALU.mult).then_inc(p_ok, 1)
                dve.wait_ge(mean_mm, b + 1)
                V.scalar_tensor_tensor(as3(yy), slot_view(g.ps[:, 0:3, :]), -1.0 / HD, as3(yy), op0=ALU.mult, op1=ALU.add).then_inc(yc_ok, 1)
                dve.wait_ge(bonus_mm, b + 1)
                if b:
                    dve.wait_ge(y2_ok, b)
                V.tensor_tensor(as3(bonus), slot_view(g.ps[:, 3:6, :]), as3(ld[:, VV, :]), op=ALU.mult).then_inc(bonus_ok, 1)
                dve.wait_ge(inv_ok, b + 1)
                dve.wait_ge(yc_ok, b + 1)
                V.tensor_tensor(yn, yy, root, op=ALU.mult).then_inc(yn_ok, 1)
                dve.wait_ge(yn_ok, b + 1)
                V.tensor_scalar(yn, yn, ch(g, "gn_w", 8 * j + b), ch(g, "gn_b", 8 * j + b), ALU.mult, ALU.add).then_inc(ya_ok, 1)
                dve.wait_ge(ya_ok, b + 1)
                dve.wait_ge(bonus_ok, b + 1)
                V.tensor_tensor(yn, yn, bonus, op=ALU.add).then_inc(y2_ok, 1)
                dve.wait_ge(y2_ok, b + 1)
                dve.wait_ge(silu_ok, b + 1)
                V.tensor_tensor(og[:, b, :], yn, sig, op=ALU.mult).then_inc(out_ok, 1)
            dve.wait_ge(out_ok, NB)

        @block.gpsimd
        def _(pool):
            for b in range(NB):
                ld = load[b % 2]
                pool.wait_ge(in_[b % 2], 256 * (b // 2 + 1))
                if b >= 2:
                    pool.wait_ge(p_ok, b - 1)
                nc.gpsimd.tensor_tensor(asum[b % 2], ld[:, A0, :], ld[:, A1, :], op=ALU.add).then_inc(as_ok, 1)
                pool.wait_ge(sig_ok, b + 1)
                nc.gpsimd.tensor_tensor(sig, sig, ld[:, GG, :], op=ALU.mult).then_inc(silu_ok, 1)


def attn_memory(g):
    rest = g.big[3].rearrange("p b t -> p (b t)")
    keys = rest[:, 0:2560].rearrange("p (b t) -> p b t", b=2)
    vals = rest[:, 2560:5120].rearrange("p (t n) -> p t n", n=256)
    wv = rest[:, 5120:7168].rearrange("p (k n) -> p k n", n=256)
    cos = rest[:, 7168:8192]
    sin = rest[:, 8192:9216]
    return keys, vals, wv, cos, sin


def phase_attention_project(nc, g):
    h, q, sg = g.big[0], g.big[1], g.big[2]
    keys, vals, wv, cos, sin = attn_memory(g)
    sq, inv, t1 = g.stage[:, 0, :], g.stage[:, 1, :], g.extra[:, 0:T]
    rot = g.extra[:, T:T + P]
    base = w_base("attn")
    V, A = nc.vector, nc.scalar
    QK = NB + 2
    with ExitStack() as ctx:
        sem = Sems(nc, ctx)
        v_in, tab_in, ctx_in, v_mm, v_ok, out_st, proj_done, sq_ok, norm_mm, rot_mm, ms_ok, root_ok, inv_ok, c_ok, s_ok, t_ok, q_ok, sig_ok, silu_ok, qw_ok = sem(
            "v_in", "tab_in", "ctx_in", "v_mm", "v_ok", "out_st", "proj_done", "sq_ok", "norm_mm", "rot_mm", "ms_ok", "root_ok",
            "inv_ok", "c_ok", "s_ok", "t_ok", "q_ok", "sig_ok", "silu_ok", "qw_ok")
        slab_in = [sem(f"slab_in{i}") for i in range(WSLOTS)]
        block = ctx.enter_context(nc.Block())
        dest = lambda n: q[:, n, :] if n < NB else keys[:, n - NB, 0:T]
        LC = LAT // 2

        @block.sync
        def _(sp):
            sp.dma_start(wv, g.io["wv"]).then_inc(v_in, 16)
            sp.dma_start(cos, g.io["cos"]).then_inc(tab_in, 16)
            sp.dma_start(sin, g.io["sin"]).then_inc(tab_in, 16)
            sp.dma_start(rot, g.io["rot"]).then_inc(tab_in, 16)
            sp.dma_start(keys[:, :, T:T + P], g.io["ck"]).then_inc(ctx_in, 16)
            sp.dma_start(vals[:, NT, :], g.io["cv"]).then_inc(ctx_in, 16)
            load_slabs(sp, g, base, 18, slab_in, proj_done)
            sp.wait_ge(q_ok, 2 * QK)
            sp.dma_start(g.io["k_out"], keys[:, :, 0:P]).then_inc(out_st, 16)
            sp.wait_ge(v_ok, 1)
            sp.dma_start(g.io["v_out"], vals[:, 0, :]).then_inc(out_st, 16)
            sp.wait_ge(out_st, 32)
            sp.wait_ge(ctx_in, 32)

        @block.tensor
        def _(pe):
            pe.wait_ge(v_in, 16)
            for t in range(NT):
                if t >= 2:
                    pe.wait_ge(v_ok, t - 1)
                for k in range(NB):
                    mm = pe.matmul(g.ps[:, 6 + t % 2, 0:256], h[:, k, t * P:(t + 1) * P], wv[:, k, :], start=k == 0, stop=k == NB - 1)
                mm.then_inc(v_mm, 1)

            def proj(n):
                pe.wait_ge(slab_in[n % WSLOTS], 16 * (n // WSLOTS + 1))
                if 1 <= n <= QK:
                    pe.wait_ge(qw_ok, n)
                    pe.wait_ge(sq_ok, n)
                elif n:
                    pe.wait_ge(silu_ok, n - QK)
                multiply(pe, g, h, n % WSLOTS, 0, proj_done)

            def norm_rot(n):
                pe.wait_ge(sq_ok, n + 1)
                if n:
                    pe.wait_ge(ms_ok, n)
                    pe.wait_ge(s_ok, n)
                for c in range(CH):
                    mm = pe.matmul(g.ps[:, 3 + c, 0:CW], g.head_ones[:, :], sq[:, c * CW:(c + 1) * CW], start=True, stop=True)
                mm.then_inc(norm_mm, 1)
                pe.wait_ge(qw_ok, n + 1)
                for c in range(2):
                    mm = pe.matmul(g.ps[:, 6 + c, :], rot, dest(n)[:, CTX + c * LC:CTX + (c + 1) * LC], start=True, stop=True)
                mm.then_inc(rot_mm, 1)

            pe.wait_ge(v_ok, NT)
            pe.wait_ge(tab_in, 48)
            for n in range(QK):
                proj(n)
                if n:
                    norm_rot(n - 1)
            proj(QK)
            norm_rot(QK - 1)
            for n in range(QK + 1, 18):
                proj(n)

        @block.scalar
        def _(act):
            for t in range(NT):
                act.wait_ge(v_mm, t + 1)
                A.copy(vals[:, t, :], g.ps[:, 6 + t % 2, 0:256]).then_inc(v_ok, 1)

            def inverse_root(n):
                act.wait_ge(ms_ok, n)
                A.activation(inv, inv, ACT.Ln).then_inc(root_ok, 1)
                act.wait_ge(root_ok, n)
                A.activation(inv, inv, ACT.Exp, scale=-0.5).then_inc(inv_ok, 1)

            for n in range(QK):
                act.wait_ge(proj_done, n + 1)
                w = ch(g, "q_norm" if n < NB else "k_norm", 0)
                A.activation(as3(dest(n)), slot_view(g.ps[:, 0:3, :]), ACT.Copy, scale=w).then_inc(qw_ok, 1)
                if n:
                    act.wait_ge(norm_mm, n)
                A.activation(as3(sq), slot_view(g.ps[:, 0:3, :]), ACT.Square).then_inc(sq_ok, 1)
                if n:
                    inverse_root(n)
            inverse_root(QK)
            for n in range(NB):
                act.wait_ge(proj_done, QK + n + 1)
                if n:
                    act.wait_ge(silu_ok, n)
                else:
                    act.wait_ge(norm_mm, QK)
                A.activation(as3(sq), slot_view(g.ps[:, 0:3, :]), ACT.Sigmoid).then_inc(sig_ok, 1)

        @block.vector
        def _(dve):
            for n in range(QK):
                dve.wait_ge(norm_mm, n + 1)
                V.tensor_scalar(as3(inv), slot_view(g.ps[:, 3:6, :]), 1.0 / HD, RMS_EPS, ALU.mult, ALU.add).then_inc(ms_ok, 1)
                dve.wait_ge(rot_mm, n + 1)
                lat = dest(n)[:, CTX:T]
                V.tensor_tensor(t1[:, 0:LAT].rearrange("p (c n) -> p c n", c=2), g.ps[:, 6:8, :],
                                sin.rearrange("p (c n) -> p c n", c=2), op=ALU.mult).then_inc(s_ok, 1)
                V.tensor_tensor(lat, lat, cos, op=ALU.mult).then_inc(c_ok, 1)
                dve.wait_ge(s_ok, n + 1)
                dve.wait_ge(c_ok, n + 1)
                V.tensor_tensor(t1[:, 0:LAT], t1[:, 0:LAT], lat, op=ALU.add).then_inc(t_ok, 1)
                dve.wait_ge(t_ok, n + 1)
                dve.wait_ge(inv_ok, n + 1)
                V.tensor_tensor(lat, t1[:, 0:LAT], inv[:, CTX:T], op=ALU.mult).then_inc(q_ok, 1)
                V.tensor_tensor(dest(n)[:, 0:CTX], dest(n)[:, 0:CTX], inv[:, 0:CTX], op=ALU.mult).then_inc(q_ok, 1)
                dve.wait_ge(q_ok, 2 * n + 2)
            for n in range(NB):
                dve.wait_ge(sig_ok, n + 1)
                V.tensor_tensor(as3(sg[:, n, :]), slot_view(g.ps[:, 0:3, :]), as3(sq), op=ALU.mult).then_inc(silu_ok, 1)
                dve.wait_ge(silu_ok, n + 1)


def phase_attention(nc, g):
    q, sg = g.big[1], g.big[2]
    keys, vals, _, _, _ = attn_memory(g)
    free = g.big[0].rearrange("p b t -> p (b t)")
    qz = [[free[:, (2 * i + h) * T:(2 * i + h + 1) * T] for h in range(2)] for i in range(2)]
    prob = [free[:, (4 + i) * T:(5 + i) * T] for i in range(2)]
    prob_t = [free[:, (6 + i) * T:(7 + i) * T] for i in range(2)]
    small = g.extra
    nmax, bias, rsum, rinv = [[small[:, 4 * k + i:4 * k + i + 1] for i in range(2)] for k in range(4)]
    V, A = nc.vector, nc.scalar
    SCALE = HD ** -0.5
    UNITS = 2 * NT
    rows = [slice(0, HD), slice(HD, P)]
    with ExitStack() as ctx:
        sem = Sems(nc, ctx)
        zero_ok, qz_ok, sc_mm, max_ok, bias_ok, exp_ok, rinv_ok, p_ok, tr_mm, tr_ok, pv_mm, o_ok = sem(
            "zero_ok", "qz_ok", "sc_mm", "max_ok", "bias_ok", "exp_ok", "rinv_ok", "p_ok", "tr_mm", "tr_ok", "pv_mm", "o_ok")
        block = ctx.enter_context(nc.Block())

        @block.gpsimd
        def _(pool):
            for i in range(2):
                for h in range(2):
                    nc.gpsimd.memset(qz[i][h], 0.0).then_inc(zero_ok, 1)
            pool.wait_ge(zero_ok, 4)
            for b in range(NB):
                i = b % 2
                if b >= 2:
                    pool.wait_ge(sc_mm, UNITS * (b - 1))
                for h in range(2):
                    nc.gpsimd.tensor_copy(qz[i][h][rows[h]], q[rows[h], b, :]).then_inc(qz_ok, 1)

        @block.tensor
        def _(pe):
            def scores(b, i, kv, u):
                t, h = u // 2, u % 2
                s = u % 2
                n = UNITS * b + u
                if u == 0:
                    pe.wait_ge(qz_ok, 2 * b + 2)
                if not isinstance(b, int) or n >= 2:
                    pe.wait_ge(tr_ok, n - 1)
                lhs = qz[i][h][:, t * P:(t + 1) * P]
                if t == 0:
                    mm = pe.matmul(g.ps[:, 3 * s, 0:P], lhs, keys[:, kv, 0:P], start=True, stop=True)
                else:
                    for c in range(CH):
                        mm = pe.matmul(g.ps[:, 3 * s + c, 0:CW], lhs, keys[:, kv, CTX + c * CW:CTX + (c + 1) * CW], start=True, stop=True)
                mm.then_inc(sc_mm, 1)

            def transposes(b, u):
                t, s = u // 2, u % 2
                n = UNITS * b + u
                pe.wait_ge(p_ok, n + 1)
                for k in range(1 if t == 0 else NT):
                    mm = pe.transpose(g.ps[:, 3 * s + k // 3, (k % 3) * P:(k % 3 + 1) * P], prob[s][:, k * P:(k + 1) * P], g.ident[:, :])
                mm.then_inc(tr_mm, 1)

            def values(b, kv, u):
                t, h = u // 2, u % 2
                n = UNITS * b + u
                pe.wait_ge(tr_ok, n + 1)
                if not isinstance(b, int) or n >= 2:
                    pe.wait_ge(o_ok, n - 1)
                nk = 1 if t == 0 else NT
                for k in range(nk):
                    tile = 0 if t == 0 else 1 + k
                    mm = pe.matmul(g.ps[rows[h], 6 + u % 2, 0:P], vals[:, tile, (2 * kv + h) * HD:(2 * kv + h + 1) * HD],
                                   prob_t[u % 2][:, k * P:(k + 1) * P], start=k == 0, stop=k == nk - 1)
                mm.then_inc(pv_mm, 1)

            def blocks(b, i, kv):
                scores(b, i, kv, 0)
                scores(b, i, kv, 1)
                for u in range(UNITS):
                    transposes(b, u)
                    if u:
                        values(b, kv, u - 1)
                    if u + 2 < UNITS:
                        scores(b, i, kv, u + 2)
                values(b, kv, UNITS - 1)

            blocks(0, 0, 0)
            blocks(1, 1, 0)
            blocks(2, 0, 0)
            blocks(3, 1, 0)
            with pe.Fori(2, 4) as r:
                for i in range(2):
                    blocks(2 * r + i, i, 1)

        def soft_loops(eng, fn):
            with eng.Fori(1, 4) as r:
                for i in range(2):
                    fn(2 * r + i, i)

        @block.scalar
        def _(act):
            def head(b, u):
                t, s = u // 2, u % 2
                n = UNITS * b + u
                act.wait_ge(bias_ok, n + 1)
                if not isinstance(b, int) or n >= 2:
                    act.wait_ge(tr_mm, n - 1)
                src = g.ps[:, 3 * s, 0:P] if t == 0 else slot_view(g.ps[:, 3 * s:3 * s + 3, :])
                dst = prob[s][:, 0:P] if t == 0 else as3(prob[s])
                A.activation(dst, src, ACT.Exp, bias=bias[s], scale=SCALE, accum_out=rsum[s]).then_inc(exp_ok, 1)

            def tail(b, u):
                t, s = u // 2, u % 2
                n = UNITS * b + u
                act.wait_ge(tr_mm, n + 1)
                if not isinstance(b, int) or n >= 2:
                    act.wait_ge(pv_mm, n - 1)
                if t == 0:
                    A.copy(prob_t[s][:, 0:P], g.ps[:, 3 * s, 0:P]).then_inc(tr_ok, 1)
                else:
                    A.copy(as3(prob_t[s]), slot_view(g.ps[:, 3 * s:3 * s + 3, :])).then_inc(tr_ok, 1)

            def blocks(b, i):
                head(b, 0)
                for u in range(UNITS):
                    tail(b, u)
                    if u + 1 < UNITS:
                        head(b, u + 1)
            blocks(0, 0)
            blocks(1, 1)
            soft_loops(act, blocks)

        @block.vector
        def _(dve):
            def head(b, u):
                t, s = u // 2, u % 2
                n = UNITS * b + u
                dve.wait_ge(sc_mm, n + 1)
                if t == 0:
                    V.tensor_reduce(nmax[s], g.ps[:, 3 * s, 0:P], mybir.AxisListType.X, ALU.max).then_inc(max_ok, 1)
                else:
                    V.tensor_reduce(nmax[s], slot_view(g.ps[:, 3 * s:3 * s + 3, :]), mybir.AxisListType.XY, ALU.max).then_inc(max_ok, 1)
                dve.wait_ge(max_ok, n + 1)
                if not isinstance(b, int) or n >= 2:
                    dve.wait_ge(exp_ok, n - 1)
                V.tensor_scalar(bias[s], nmax[s], -SCALE, None, ALU.mult).then_inc(bias_ok, 1)

            def mid(b, u):
                t, s = u // 2, u % 2
                n = UNITS * b + u
                w = P if t == 0 else T
                dve.wait_ge(exp_ok, n + 1)
                V.reciprocal(rinv[s], rsum[s]).then_inc(rinv_ok, 1)
                dve.wait_ge(rinv_ok, n + 1)
                V.tensor_scalar(prob[s][:, 0:w], prob[s][:, 0:w], rinv[s], None, ALU.mult).then_inc(p_ok, 1)

            def tail(b, u):
                t, h = u // 2, u % 2
                n = UNITS * b + u
                dve.wait_ge(pv_mm, n + 1)
                gate = (sg[rows[h], b, t * P:(t + 1) * P] if isinstance(b, int)
                        else sg[rows[h], bass.ds(b, 1), t * P:(t + 1) * P].rearrange("p o n -> p (o n)"))
                V.tensor_tensor(gate, g.ps[rows[h], 6 + u % 2, 0:P], gate, op=ALU.mult).then_inc(o_ok, 1)

            def blocks(b, i):
                head(b, 0)
                mid(b, 0)
                for u in range(UNITS):
                    if u + 1 < UNITS:
                        head(b, u + 1)
                    if u >= 2:
                        tail(b, u - 2)
                    if u + 1 < UNITS:
                        mid(b, u + 1)
                tail(b, UNITS - 2)
                tail(b, UNITS - 1)
            blocks(0, 0)
            blocks(1, 1)
            soft_loops(dve, blocks)
            dve.wait_ge(o_ok, NB * UNITS)


def phase_conv(nc, g):
    h, og = g.big[0], g.big[1]
    t = g.big[2]
    H_LOW, H_HIGH = 0, 3
    cs, uu, cv, gg, sig = [t[:, i, :] for i in range(5)]
    V, A = nc.vector, nc.scalar
    with ExitStack() as ctx:
        sem = Sems(nc, ctx)
        proj_done, evacuated, c_ok, u_ok, w1_ok, w0_ok, w2_ok, b_ok, sig_ok, silu_ok, out_ok = sem(
            "proj_done", "evacuated", "c_ok", "u_ok", "w1_ok", "w0_ok", "w2_ok", "b_ok", "sig_ok", "silu_ok", "out_ok")
        high_ok, low_ok, rows_high_ok, rows_ok = sem("high_ok", "low_ok", "rows_high_ok", "rows_ok")
        slab_in = [sem(f"slab_in{i}") for i in range(WSLOTS)]
        block = ctx.enter_context(nc.Block())

        @block.sync
        def _(sp):
            load_slabs(sp, g, w_base("conv"), 4 * NB, slab_in, proj_done)

        @block.tensor
        def _(pe):
            def block_of(b, first=False):
                for u in range(4):
                    pe.wait_ge(low_ok, 4 * b + u + 1)
                    if u == 2:
                        pe.wait_ge(c_ok, b + 1)
                    elif u == 3:
                        pe.wait_ge(evacuated, 3 * b + 1)
                    elif not first:
                        pe.wait_ge(evacuated, 3 * b - 1 + u)
                    multiply_split(pe, g, H_HIGH, H_LOW, u % 2, 3 * (u % 2), proj_done, rows_ok if first and u == 0 else None)
            block_of(0, True)
            with pe.Fori(1, NB) as b:
                block_of(b)

        @block.scalar
        def _(act):
            for b in range(NB):
                act.wait_ge(proj_done, 4 * b + 1)
                if b:
                    act.wait_ge(u_ok, b)
                A.copy(as3(cs), slot_view(g.ps[:, 0:3, :])).then_inc(c_ok, 1)
                act.wait_ge(proj_done, 4 * b + 4)
                if b:
                    act.wait_ge(silu_ok, b)
                A.activation(as3(sig), slot_view(g.ps[:, 3:6, :]), ACT.Sigmoid).then_inc(sig_ok, 1)

        @block.gpsimd
        def _(pool):
            split_slabs(nc, g, pool, 4 * NB, high_ok, low_ok)

        @block.vector
        def _(dve):
            def next_slab(n):
                if n < 4 * NB:
                    high_slab(nc, g, dve, n, slab_in, proj_done, high_ok)

            next_slab(0)
            split_rows(nc, g, dve, H_HIGH, H_LOW, rows_high_ok, rows_ok)
            next_slab(1)
            for b in range(NB):
                dve.wait_ge(proj_done, 4 * b + 1)
                next_slab(4 * b + 2)
                w = lambda i: ch(g, "conv_w", 8 * i + b)
                dve.wait_ge(proj_done, 4 * b + 2)
                dve.wait_ge(c_ok, b + 1)
                V.tensor_tensor(as3(uu), slot_view(g.ps[:, 3:6, :]), as3(cs), op=ALU.mult).then_inc(evacuated, 1)
                next_slab(4 * b + 3)
                dve.wait_ge(evacuated, 3 * b + 1)
                V.tensor_scalar(cv, uu, w(1), ch(g, "conv_b", b), ALU.mult, ALU.add).then_inc(w1_ok, 1)
                dve.wait_ge(w1_ok, b + 1)
                for _, a0, a1 in token_ranges():
                    V.scalar_tensor_tensor(cv[:, a0 + 1:a1], uu[:, a0:a1 - 1], w(0), cv[:, a0 + 1:a1], op0=ALU.mult, op1=ALU.add).then_inc(w0_ok, 1)
                dve.wait_ge(w0_ok, 2 * b + 2)
                for i, (_, a0, a1) in enumerate(token_ranges()):
                    V.scalar_tensor_tensor(cv[:, a0:a1 - 1], uu[:, a0 + 1:a1], w(2), cv[:, a0:a1 - 1], op0=ALU.mult, op1=ALU.add).then_inc(w2_ok, 1)
                dve.wait_ge(w2_ok, 2 * b + 2)
                V.tensor_copy(g.flag[:, 2:3], g.flag[:, 1:2]).then_inc(u_ok, 1)
                dve.wait_ge(proj_done, 4 * b + 3)
                V.tensor_tensor(as3(cv), slot_view(g.ps[:, 0:3, :]), as3(cv), op=ALU.mult).then_inc(evacuated, 1)
                next_slab(4 * b + 4)
                dve.wait_ge(evacuated, 3 * b + 2)
                dve.wait_ge(sig_ok, b + 1)
                V.tensor_tensor(as3(gg), slot_view(g.ps[:, 3:6, :]), as3(sig), op=ALU.mult).then_inc(evacuated, 1)
                next_slab(4 * b + 5)
                dve.wait_ge(evacuated, 3 * b + 3)
                dve.wait_ge(u_ok, b + 1)
                V.tensor_tensor(og[:, b, :], cv, gg, op=ALU.mult).then_inc(silu_ok, 1)
                dve.wait_ge(silu_ok, b + 1)


def residual(nc, g, ada, tmp, b, x_ok):
    for c, a0, a1 in token_ranges():
        nc.vector.scalar_tensor_tensor(g.x[:, b, a0:a1], tmp[:, b, a0:a1], ada[:, 16 + b, c:c + 1], g.x[:, b, a0:a1],
                                       op0=ALU.mult, op1=ALU.add).then_inc(x_ok, 1)


def phase_output(nc, g, layer):
    kind = MIXER[layer]
    og_at, tmp_at = ((0, 1), (2, 0), (1, 0))[kind]
    og = g.big[og_at]
    base = (w_base("rwkv", layer // 3) + W_RWKV, w_base("attn") + 18, w_base("conv") + 32)[kind]
    m = g.big[3]
    tmp = g.big[tmp_at]
    work = (g.big[2], g.big[1], g.big[2])[kind]
    sq = [work[:, i, :] for i in range(2)]
    acc = work[:, 5, :]
    ms, root, rstd = work[:, 2, :], work[:, 3, :], work[:, 4, :]
    ada = g.ada[:, layer]
    V, A = nc.vector, nc.scalar
    with ExitStack() as ctx:
        sem = Sems(nc, ctx)
        proj_done, evacuated, sq_ok, zero_ok, acc_ok, sum_mm, ms_ok, root_ok, rstd_ok, tmp_ok, x_ok = sem(
            "proj_done", "evacuated", "sq_ok", "zero_ok", "acc_ok", "sum_mm", "ms_ok", "root_ok", "rstd_ok", "tmp_ok", "x_ok")
        high_ok, low_ok, rows_high_ok, rows_ok = sem("high_ok", "low_ok", "rows_high_ok", "rows_ok")
        slab_in = [sem(f"slab_in{i}") for i in range(WSLOTS)]
        block = ctx.enter_context(nc.Block())

        @block.sync
        def _(sp):
            load_slabs(sp, g, base, NB, slab_in, proj_done)

        @block.tensor
        def _(pe):
            project(pe, g, og, NB, 0, slab_in, evacuated, proj_done, (tmp_at, og_at, low_ok, rows_ok))
            pe.wait_ge(evacuated, NB)
            pe.wait_ge(acc_ok, NB)
            for c in range(CH):
                mm = pe.matmul(g.ps[:, c, 0:CW], g.ones[:, :], acc[:, c * CW:(c + 1) * CW], start=True, stop=True)
            mm.then_inc(sum_mm, 1)

        @block.scalar
        def _(act):
            for b in range(NB):
                act.wait_ge(proj_done, b + 1)
                A.copy(as3(m[:, b, :]), slot_view(g.ps[:, 3 * (b % 2):3 * (b % 2) + 3, :])).then_inc(evacuated, 1)
                act.wait_ge(evacuated, b + 1)
                if b >= 2:
                    act.wait_ge(acc_ok, b - 1)
                A.activation(sq[b % 2], m[:, b, :], ACT.Square).then_inc(sq_ok, 1)
            act.wait_ge(ms_ok, 1)
            A.activation(root, ms, ACT.Ln).then_inc(root_ok, 1)
            act.wait_ge(root_ok, 1)
            A.activation(rstd, root, ACT.Exp, scale=-0.5).then_inc(rstd_ok, 1)

        @block.gpsimd
        def _(pool):
            split_slabs(nc, g, pool, NB, high_ok, low_ok)

        @block.vector
        def _(dve):
            high_slab(nc, g, dve, 0, slab_in, proj_done, high_ok)
            split_rows(nc, g, dve, tmp_at, og_at, rows_high_ok, rows_ok)
            high_slab(nc, g, dve, 1, slab_in, proj_done, high_ok)
            V.memset(acc, 0.0).then_inc(zero_ok, 1)
            dve.wait_ge(zero_ok, 1)
            for b in range(NB):
                if b + 2 < NB:
                    high_slab(nc, g, dve, b + 2, slab_in, proj_done, high_ok)
                dve.wait_ge(sq_ok, b + 1)
                if b:
                    dve.wait_ge(acc_ok, b)
                V.tensor_tensor(acc, acc, sq[b % 2], op=ALU.add).then_inc(acc_ok, 1)
            dve.wait_ge(sum_mm, 1)
            V.tensor_scalar(as3(ms), slot_view(g.ps[:, 0:3, :]), 1.0 / D, RMS_EPS, ALU.mult, ALU.add).then_inc(ms_ok, 1)
            dve.wait_ge(rstd_ok, 1)
            for b in range(NB):
                V.tensor_tensor(tmp[:, b, :], m[:, b, :], rstd, op=ALU.mult).then_inc(tmp_ok, 1)
                if b:
                    dve.wait_ge(tmp_ok, b)
                    residual(nc, g, ada, tmp, b - 1, x_ok)
            dve.wait_ge(tmp_ok, NB)
            residual(nc, g, ada, tmp, NB - 1, x_ok)
            dve.wait_ge(x_ok, 2 * NB)


def phase_end(nc, g):
    with ExitStack() as ctx:
        stored = Sems(nc, ctx)("stored_y")
        block = ctx.enter_context(nc.Block())

        @block.sync
        def _(sp):
            sp.dma_start(g.io["y"], g.x[:, :, :]).then_inc(stored, 16)
            sp.wait_ge(stored, 16)


def constants():
    t = np.arange(P)
    row, col = t[:, None], t[None, :]
    out = {}
    masks = np.zeros((P, len(MASKS), 2, P), np.float32)

    def put(name, fwd, bwd):
        masks[:, MASKS[name], 0] = fwd
        masks[:, MASKS[name], 1] = bwd
    put("strict", row < col, row > col)
    put("incl", row <= col, row >= col)
    for k in range(LEVELS):
        n = 1 << k
        low = (row // n == col // n + 1) & ((row // n) % 2 == 1)
        if k == 0:
            put("lv0t", low.T, low)
        elif k < LEVELS - 1:
            put(f"lv{k}", low, low.T)
    put("eye", row == col, row == col)
    out["masks"] = masks
    reset = np.ones((P, 4, P), np.float32)
    reset[:, :, 0] = 0
    out["reset"] = reset.reshape(P, 4 * P)
    out["ident"] = np.eye(P, dtype=np.float32)
    out["ones"] = np.ones((P, P), np.float32)
    out["head_ones"] = (row // HD == col // HD).astype(np.float32)
    f = HD // 4
    inv = np.float32(10000.0) ** (-np.arange(f, dtype=np.float32) / np.float32(f))
    pos = np.arange(LAT)
    axis = np.stack([pos // 64, pos % 64]).astype(np.float32)
    d = np.arange(P) % HD
    ang = axis[d // 32] * inv[d % f][:, None]
    out["cos"] = np.cos(ang).astype(np.float32)
    out["sin"] = np.sin(ang).astype(np.float32)
    rot = np.zeros((P, P), np.float32)
    for c in range(P):
        if (c % 32) < f:
            rot[c + f, c] = -1
        else:
            rot[c - f, c] = 1
    out["rot"] = rot
    return out


def columns(v):
    return np.asarray(v).reshape(-1, P).T


def slabs(w):
    e = w.shape[1]
    return w.reshape(NB, P, e // P, P).transpose(2, 1, 0, 3).reshape(e // P, P, NB * P)


def layout(i):
    f = {k: np.asarray(v) for k, v in i.items()}
    io = constants()
    x = np.concatenate([f["x_prompt"][0], f["x_sample"][0]])
    io["x"] = x.T.reshape(NB, P, T).transpose(1, 0, 2)
    io["cond"] = np.stack([f["c_ctx"], f["c"][0]], -1).reshape(NB, P, 2).transpose(1, 0, 2)
    io["w_ada"] = f["w_ada"].reshape(4, NB, P, 6, 512).transpose(0, 3, 2, 1, 4).reshape(24, P, NB, 512)
    hd = np.tile(f["attn_q_norm"][0], 2)[:, None], np.tile(f["attn_k_norm"][0], 2)[:, None]
    parts = dict(norm_pre=columns(f["norm_pre"]), norm_post=columns(f["norm_post"]), b_ada=columns(f["b_ada"]), mu=columns(f["rwkv_mu"]),
                 decay0=columns(f["rwkv_decay0"]), icl0=columns(f["rwkv_icl0"]), k_k=columns(f["rwkv_k_k"]), r_k=columns(f["rwkv_r_k"]),
                 gn_w=columns(f["rwkv_gn_w"]), gn_b=columns(f["rwkv_gn_b"]), k_a=columns(f["rwkv_k_a"]), q_norm=hd[0], k_norm=hd[1],
                 conv_w=columns(f["conv_w"]), conv_b=columns(f["conv_b"]))
    lay = chan_layout()
    io["chan"] = np.concatenate([parts[n] for n in lay if n != "_"], 1)
    order = [h for b in range(4) for h in (b, 4 + b)] + [h for b in range(4) for h in (8 + b, 12 + b)]
    cols = np.concatenate([np.arange(h * HD, (h + 1) * HD) for h in order])
    wi = f["attn_w_in"][0]
    w = []
    for j in range(2):
        w += [slabs(f["rwkv_w_in"][j, m]) for m in range(4)]
        w += [slabs(f[n][j].transpose(1, 0, 2).reshape(D, P)) for n in ("rwkv_decay1", "rwkv_icl1")]
        w.append(slabs(f["rwkv_w_out"][j]))
    w += [slabs(wi[:, cols]), slabs(wi[:, D:D + 256]), slabs(wi[:, D + 512:][:, cols]), slabs(f["attn_w_out"][0][cols])]
    cw = np.stack([slabs(f["conv_w_in"][0][:, a * D:(a + 1) * D]) for a in (1, 2, 0, 3)], 1)
    w += [cw.reshape(4 * NB, P, NB * P), slabs(f["conv_w_out"][0])]
    io["w"] = np.concatenate(w)
    up = np.zeros((2, P, 2, 2, NB, P), np.float32)
    for a, n in enumerate(("rwkv_decay2", "rwkv_icl2")):
        for z in range(2):
            up[:, z * 64:(z + 1) * 64, a, z] = f[n][:, z].reshape(2, 64, NB, P)
    io["lora_up"] = up.reshape(2, P, 32, P)
    io["wv"] = wi[:, D + 256:D + 512].reshape(NB, P, 256).transpose(1, 0, 2)
    io["ck"] = f["cache_k"][0, 0].reshape(P, 2, P).transpose(2, 1, 0)
    io["cv"] = f["cache_v"][0, 0].reshape(P, 256)
    st = f["state_rwkv"][0].transpose(0, 1, 2, 4, 3).reshape(2, 2, NB, P, HD)
    io["state_in"] = np.stack([st[:, 0], st[:, 1, ::-1]], 3)
    ka = f["rwkv_k_a"].reshape(2, NB, P)
    both = np.stack([ka, ka[:, ::-1]], -1)
    both = np.tile(both.reshape(2, 4, 2, P, 2), (1, NT, 1, 1, 1))
    io["ka"] = both.transpose(0, 1, 3, 2, 4).reshape(2, PAIRS, P, 4)
    return {k: np.ascontiguousarray(v) for k, v in io.items()}


OUTS = {"y": (P, NB, T), "state_out": (2, NB, P, 2, HD), "k_out": (P, 2, P), "v_out": (P, 256)}


def program(nc, arrays, **kw):
    io = {k: nc.dram_tensor(f"in_{k}", a.shape, F32, kind="ExternalInput").ap() for k, a in arrays.items()}
    io.update({k: nc.dram_tensor(f"out_{k}", s, F32, kind="ExternalOutput").ap() for k, s in OUTS.items()})
    build(nc, io, **kw)


def unpack(r):
    y = r["out_y"].transpose(1, 0, 2).reshape(D, T).T
    st = r["out_state_out"]
    fwd, bwd = st[:, :, :, 0], st[:, ::-1, :, 1]
    both = np.stack([fwd, bwd], 1).reshape(2, 2, 16, HD, HD).transpose(0, 1, 2, 4, 3)
    k = r["out_k_out"].transpose(2, 1, 0).reshape(1, 1, CTX, 4, HD)
    v = r["out_v_out"].reshape(1, 1, CTX, 4, HD)
    c = np.ascontiguousarray
    return c(y[None, :CTX]), c(y[None, CTX:]), c(both[None]), c(k), c(v)


def kernel(**inputs):
    import concourse.bacc as bacc
    from concourse.bass_utils import run_bass_kernel_spmd as run
    nc = bacc.Bacc("TRN2", target_bir_lowering=False, num_devices=1)
    arrays = layout(inputs)
    program(nc, arrays)
    r = run(nc, [{f"in_{k}": a for k, a in arrays.items()}], core_ids=[0])
    return unpack(r.results[0])
```
